# Optimizing a Trainium2 kernel written in Bass

```python
import jax, jax.numpy as jnp
from jax import lax
import numpy as np

D_MODEL = 1024
BATCH = 1
SEQ = 256
DEPTH = 2

GRID_W = 64
CTX_LEN = 256
N_EVEN = (DEPTH + 1) // 2
N_ODD = DEPTH // 2
EPS = 1e-6
ADA_SCALE = 0.3

CONV_CH = D_MODEL // 2
CONV_W = 3
HEAD_DIM = 64
N_Q_HEADS = (D_MODEL // 2) // HEAD_DIM
N_KV_HEADS = 2
GQA_GROUP = N_Q_HEADS // N_KV_HEADS
Q_DIM = N_Q_HEADS * HEAD_DIM
KV_DIM = N_KV_HEADS * HEAD_DIM
WINDOW = 128
ATT_BLOCK = 128
ROPE_BASE = 10000.0
ROPE_PAIRS = HEAD_DIM // 4
AB_SPLITS = [CONV_CH, 2 * CONV_CH, 3 * CONV_CH, 3 * CONV_CH + Q_DIM, 3 * CONV_CH + Q_DIM + KV_DIM]
KV_OFF = 3 * CONV_CH + Q_DIM
AB_IN = 3 * CONV_CH + Q_DIM + 2 * KV_DIM
AB_OUT = CONV_CH + Q_DIM
D_FF = 2816
D_INNER = 2 * D_MODEL
SSD_HEADDIM = 64
SSD_HEADS = D_INNER // SSD_HEADDIM
SSD_GROUPS = 4
SSD_REP = SSD_HEADS // SSD_GROUPS
SSD_STATE = 128
SSD_CHUNK = 128
SSD_CONV_W = 3
GN_DIM = SSD_GROUPS * SSD_STATE
XB_DIM = D_INNER + GN_DIM
SSD_CONV_DIM = D_INNER + 2 * GN_DIM
DT_OFF = D_INNER + SSD_CONV_DIM
SSD_IN = DT_OFF + 2 * SSD_HEADS
N_EXPERTS = 8
TOP_K = 2
D_FF_EXPERT = 3584

kernel_name = "hybrid_conv_swa_ssd_moe_dit_block"

def rmsnorm(x, g):
    xf = x.astype(jnp.float32)
    y = xf * lax.rsqrt(jnp.mean(xf * xf, axis=-1, keepdims=True) + EPS)
    return y.astype(x.dtype) * g

def modulate(x, g, shift, scale):
    return rmsnorm(x, g) * (1 + scale) + shift

def conv_centered(u, w, bias=None):
    k_w = w.shape[0]
    pad = k_w // 2
    L = u.shape[1]
    up = jnp.pad(u, ((0, 0), (pad, pad), (0, 0)))
    y = up[:, 0:L] * w[0]
    for k in range(1, k_w):
        y = y + up[:, k:k + L] * w[k]
    if bias is not None:
        y = y + bias
    return y

def heads(t, n):
    return t.reshape(t.shape[:2] + (n, HEAD_DIM))

def rope2d_tables(L):
    rows = L // GRID_W
    row = jnp.repeat(jnp.arange(rows, dtype=jnp.float32), GRID_W)
    col = jnp.tile(jnp.arange(GRID_W, dtype=jnp.float32), rows)
    inv = ROPE_BASE ** (-jnp.arange(ROPE_PAIRS, dtype=jnp.float32) / ROPE_PAIRS)
    ang = jnp.stack([row, col], axis=-1)[..., None] * inv
    return jnp.cos(ang), jnp.sin(ang)

def apply_rope2d(x, cos, sin):
    b, L, H, _ = x.shape
    xr = x.reshape(b, L, H, 2, 2, ROPE_PAIRS)
    x1, x2 = xr[..., 0, :], xr[..., 1, :]
    cs, sn = cos[:, None], sin[:, None]
    out = jnp.stack([x1 * cs - x2 * sn, x2 * cs + x1 * sn], axis=-2)
    return out.reshape(x.shape).astype(x.dtype)

def short_conv_mixer(g_b, g_c, h_a, conv_w):
    return g_b * conv_centered(g_c * h_a, conv_w)

def sink_column(sink, shape):
    s = sink.astype(jnp.float32).reshape((1,) * (len(shape) - 4) + (N_KV_HEADS, GQA_GROUP, 1, 1))
    return jnp.broadcast_to(s, shape[:-1] + (1,))

def context_attention(q, k, v, sink):
    b, lc = q.shape[:2]
    qg = q.reshape(b, lc, N_KV_HEADS, GQA_GROUP, HEAD_DIM)
    s = jnp.einsum('bqhgd,bkhd->bhgqk', qg, k).astype(jnp.float32) * (HEAD_DIM ** -0.5)
    s = jnp.concatenate([s, sink_column(sink, s.shape)], axis=-1)
    p = jax.nn.softmax(s, axis=-1)[..., :-1].astype(v.dtype)
    return jnp.einsum('bhgqk,bkhd->bqhgd', p, v).reshape(b, lc, Q_DIM)

def windowed_attention(q, k, v, kc, vc, sink):
    b, L = q.shape[:2]
    lc = kc.shape[1]
    nb = L // ATT_BLOCK
    qb = q.reshape(b, nb, ATT_BLOCK, N_KV_HEADS, GQA_GROUP, HEAD_DIM)

    def band(t):
        tp = jnp.pad(t, ((0, 0), (ATT_BLOCK, ATT_BLOCK), (0, 0), (0, 0)))
        tp = tp.reshape(b, nb + 2, ATT_BLOCK, N_KV_HEADS, HEAD_DIM)
        return jnp.concatenate([tp[:, :-2], tp[:, 1:-1], tp[:, 2:]], axis=2)

    kb, vb = band(k), band(v)
    scale = HEAD_DIM ** -0.5
    s_loc = jnp.einsum('bnqhgd,bnkhd->bnhgqk', qb, kb).astype(jnp.float32) * scale
    s_ctx = jnp.einsum('bnqhgd,bchd->bnhgqc', qb, kc).astype(jnp.float32) * scale
    blk = jnp.arange(nb)[:, None, None]
    qpos = blk * ATT_BLOCK + jnp.arange(ATT_BLOCK)[None, :, None]
    kpos = (blk - 1) * ATT_BLOCK + jnp.arange(3 * ATT_BLOCK)[None, None, :]
    valid = (jnp.abs(qpos - kpos) <= WINDOW) & (kpos >= 0) & (kpos < L)
    s_loc = jnp.where(valid[None, :, None, None], s_loc, -jnp.inf)
    logits = jnp.concatenate([s_loc, s_ctx, sink_column(sink, s_loc.shape)], axis=-1)
    p = jax.nn.softmax(logits, axis=-1).astype(v.dtype)
    n_loc = 3 * ATT_BLOCK
    o = (jnp.einsum('bnhgqk,bnkhd->bnqhgd', p[..., :n_loc], vb)
         + jnp.einsum('bnhgqc,bchd->bnqhgd', p[..., n_loc:n_loc + lc], vc))
    return o.reshape(b, L, Q_DIM)

def mixer_ab(h, hc, w_in, conv_w, sink, w_out, cos, sin, last):
    if last:
        kc, vc = jnp.split(hc @ w_in[:, KV_OFF:], [KV_DIM], axis=-1)
    else:
        gbc, gcc, hac, qc, kc, vc = jnp.split(hc @ w_in, AB_SPLITS, axis=-1)
    kc, vc = heads(kc, N_KV_HEADS), heads(vc, N_KV_HEADS)
    g_b, g_c, h_a, q, k, v = jnp.split(h @ w_in, AB_SPLITS, axis=-1)
    a_out = short_conv_mixer(g_b, g_c, h_a, conv_w)
    q = apply_rope2d(heads(q, N_Q_HEADS), cos, sin)
    k = apply_rope2d(heads(k, N_KV_HEADS), cos, sin)
    att = windowed_attention(q, k, heads(v, N_KV_HEADS), kc, vc, sink)
    y = jnp.concatenate([a_out, att], axis=-1) @ w_out
    if last:
        return y, None
    ac = short_conv_mixer(gbc, gcc, hac, conv_w)
    attc = context_attention(heads(qc, N_Q_HEADS), kc, vc, sink)
    yc = jnp.concatenate([ac, attc], axis=-1) @ w_out
    return y, yc

def split_xb(xb):
    b, L = xb.shape[:2]
    xs, bm = jnp.split(xb, [D_INNER], axis=-1)
    return xs.reshape(b, L, SSD_HEADS, SSD_HEADDIM), bm.reshape(b, L, SSD_GROUPS, SSD_STATE)

def dt_from(dt_raw, bias_f, bias_b):
    d = dt_raw.astype(jnp.float32)
    return (jax.nn.softplus(d[..., :SSD_HEADS] + bias_f.astype(jnp.float32)),
            jax.nn.softplus(d[..., SSD_HEADS:] + bias_b.astype(jnp.float32)))

def ssd_features(p, conv_w, conv_b, dtb_f, dtb_b):
    z, xbc, dt_raw = jnp.split(p, [D_INNER, DT_OFF], axis=-1)
    xbc = jax.nn.silu(conv_centered(xbc, conv_w, conv_b))
    xs, bm = split_xb(xbc[..., :XB_DIM])
    cm = xbc[..., XB_DIM:].reshape(p.shape[:2] + (SSD_GROUPS, SSD_STATE))
    dt_f, dt_b = dt_from(dt_raw, dtb_f, dtb_b)
    return z, xs, bm, cm, dt_f, dt_b

def ssd_scan(x, dt, a_coef, bm, cm, init):
    f32 = jnp.float32
    b, L = x.shape[:2]
    nc, q = L // SSD_CHUNK, SSD_CHUNK
    a = (dt * a_coef).reshape(b, nc, q, SSD_GROUPS, SSD_REP).transpose(0, 1, 3, 4, 2)
    a_cum = jnp.cumsum(a, axis=-1)
    xdt = (x.astype(f32) * dt[..., None]).reshape(b, nc, q, SSD_GROUPS, SSD_REP, SSD_HEADDIM)
    bc = bm.astype(f32).reshape(b, nc, q, SSD_GROUPS, SSD_STATE)
    cc = cm.astype(f32).reshape(b, nc, q, SSD_GROUPS, SSD_STATE)
    causal = jnp.tril(jnp.ones((q, q), dtype=bool))
    lmat = jnp.exp(jnp.where(causal, a_cum[..., :, None] - a_cum[..., None, :], -jnp.inf))
    cb = jnp.einsum('bclgn,bcsgn->bcgls', cc, bc)
    y_diag = jnp.einsum('bcgrls,bcsgrp->bclgrp', cb[:, :, :, None] * lmat, xdt)
    decay_end = jnp.exp(a_cum[..., -1:] - a_cum).transpose(0, 1, 4, 2, 3)
    chunk_states = jnp.einsum('bclgn,bclgrp->bcgrpn', bc, xdt * decay_end[..., None])
    chunk_decay = jnp.exp(a_cum[..., -1])

    def step(state, inp):
        dec, st = inp
        return state * dec[..., None, None] + st, state

    final, prev = lax.scan(step, init.astype(f32),
                           (jnp.moveaxis(chunk_decay, 1, 0), jnp.moveaxis(chunk_states, 1, 0)))
    prev = jnp.moveaxis(prev, 0, 1)
    decay_in = jnp.exp(a_cum).transpose(0, 1, 4, 2, 3)[..., None]
    y_off = jnp.einsum('bclgn,bcgrpn->bclgrp', cc, prev) * decay_in
    return (y_diag + y_off).reshape(b, L, SSD_HEADS, SSD_HEADDIM), final

def ssd_final_state(x, dt, a_coef, bm):
    b, L = x.shape[:2]
    a_cum = jnp.cumsum(dt * a_coef, axis=1)
    w = dt * jnp.exp(a_cum[:, -1:] - a_cum)
    xw = (x.astype(jnp.float32) * w[..., None]).reshape(b, L, SSD_GROUPS, SSD_REP, SSD_HEADDIM)
    return jnp.einsum('blgn,blgrp->bgrpn', bm.astype(jnp.float32), xw)

def flip(t):
    return jnp.flip(t, axis=1)

def ssd_bidirectional(xs, bm, cm, dt_f, dt_b, a_f, a_b, init_f, init_b):
    y_f, s_f = ssd_scan(xs, dt_f, a_f, bm, cm, init_f)
    y_b, s_b = ssd_scan(flip(xs), flip(dt_b), a_b, flip(bm), flip(cm), init_b)
    return y_f + flip(y_b), s_f, s_b

def ssd_output(y, xs, z, d_skip, norm_g, w_out):
    b, L = y.shape[:2]
    y = y + xs.astype(jnp.float32) * d_skip.astype(jnp.float32)[:, None]
    gshape = (b, L, SSD_GROUPS, D_INNER // SSD_GROUPS)
    y = y.reshape(gshape) * jax.nn.silu(z.astype(jnp.float32)).reshape(gshape)
    y = y * lax.rsqrt(jnp.mean(y * y, axis=-1, keepdims=True) + EPS)
    return (y.reshape(b, L, D_INNER).astype(z.dtype) * norm_g) @ w_out

def mixer_ssd(h, hc, w_in, conv_w, conv_b, dtb_f, dtb_b, alog_f, alog_b, d_skip, norm_g, w_out, last):
    a_f = -jnp.exp(alog_f.astype(jnp.float32))
    a_b = -jnp.exp(alog_b.astype(jnp.float32))
    b = h.shape[0]
    if last:
        xb_c = jax.nn.silu(conv_centered(hc @ w_in[:, D_INNER:D_INNER + XB_DIM],
                                         conv_w[:, :XB_DIM], conv_b[:XB_DIM]))
        xs_c, b_c = split_xb(xb_c)
        dtf_c, dtb_c = dt_from(hc @ w_in[:, DT_OFF:], dtb_f, dtb_b)
        s_f = ssd_final_state(xs_c, dtf_c, a_f, b_c)
        s_b = ssd_final_state(flip(xs_c), flip(dtb_c), a_b, flip(b_c))
        yc = None
    else:
        z_c, xs_c, b_c, c_c, dtf_c, dtb_c = ssd_features(hc @ w_in, conv_w, conv_b, dtb_f, dtb_b)
        zero = jnp.zeros((b, SSD_GROUPS, SSD_REP, SSD_HEADDIM, SSD_STATE), jnp.float32)
        y_c, s_f, s_b = ssd_bidirectional(xs_c, b_c, c_c, dtf_c, dtb_c, a_f, a_b, zero, zero)
        yc = ssd_output(y_c, xs_c, z_c, d_skip, norm_g, w_out)
    z, xs, bm, cm, dt_f, dt_b = ssd_features(h @ w_in, conv_w, conv_b, dtb_f, dtb_b)
    y, _, _ = ssd_bidirectional(xs, bm, cm, dt_f, dt_b, a_f, a_b, s_f, s_b)
    return ssd_output(y, xs, z, d_skip, norm_g, w_out), yc

def swiglu(h, wg, wu, wd):
    return (jax.nn.silu(h @ wg) * (h @ wu)) @ wd

def moe_ffn(h, router, wg, wu, wd):
    logits = (h @ router).astype(jnp.float32)
    top_v, top_i = lax.top_k(logits, TOP_K)
    w = jax.nn.softmax(top_v, axis=-1)
    gates = jnp.einsum('btk,btke->bte', w, jax.nn.one_hot(top_i, N_EXPERTS, dtype=jnp.float32)).astype(h.dtype)
    out = jnp.zeros_like(h)
    for e in range(N_EXPERTS):
        out = out + gates[..., e:e + 1] * swiglu(h, wg[e], wu[e], wd[e])
    return out

def setup_inputs(seed: int = 0) -> dict:
    key = jax.random.key(seed)
    ks = iter(jax.random.split(key, 40))
    f32 = jnp.float32

    def nrm(shape, scale):
        return jax.random.normal(next(ks), shape, f32) * scale

    def gain(shape):
        return 1.0 + nrm(shape, 0.02)

    def dt_bias(shape):
        u = jax.random.uniform(next(ks), shape, f32)
        dt = jnp.exp(u * (np.log(0.1) - np.log(0.001)) + np.log(0.001)).astype(f32)
        return dt + jnp.log(-jnp.expm1(-dt))

    def a_log(shape):
        return jnp.log(jax.random.uniform(next(ks), shape, f32, minval=1.0, maxval=16.0))

    D = D_MODEL
    return {
        "x": nrm((BATCH, SEQ, D), 1.0),
        "c": nrm((BATCH, D), 1.0),
        "ctx": nrm((BATCH, CTX_LEN, D), 1.0),
        "c_ctx": nrm((D,), 1.0),
        "ada_w": nrm((DEPTH, D, 6 * D), ADA_SCALE * D ** -0.5),
        "ada_b": nrm((DEPTH, 6 * D), 0.02),
        "norm1_g": gain((DEPTH, D)),
        "norm2_g": gain((DEPTH, D)),
        "ab_w_in": nrm((N_EVEN, D, AB_IN), D ** -0.5),
        "ab_conv_w": nrm((N_EVEN, CONV_W, CONV_CH), CONV_W ** -0.5),
        "ab_sink": nrm((N_EVEN, N_Q_HEADS), 0.5),
        "ab_w_out": nrm((N_EVEN, AB_OUT, D), AB_OUT ** -0.5),
        "ffn_w_gate": nrm((N_EVEN, D, D_FF), D ** -0.5),
        "ffn_w_up": nrm((N_EVEN, D, D_FF), D ** -0.5),
        "ffn_w_down": nrm((N_EVEN, D_FF, D), D_FF ** -0.5),
        "ssd_w_in": nrm((N_ODD, D, SSD_IN), D ** -0.5),
        "ssd_conv_w": nrm((N_ODD, SSD_CONV_W, SSD_CONV_DIM), SSD_CONV_W ** -0.5),
        "ssd_conv_b": nrm((N_ODD, SSD_CONV_DIM), 0.02),
        "ssd_dt_bias_f": dt_bias((N_ODD, SSD_HEADS)),
        "ssd_dt_bias_b": dt_bias((N_ODD, SSD_HEADS)),
        "ssd_a_log_f": a_log((N_ODD, SSD_HEADS)),
        "ssd_a_log_b": a_log((N_ODD, SSD_HEADS)),
        "ssd_d": gain((N_ODD, SSD_HEADS)),
        "ssd_norm_g": gain((N_ODD, D_INNER)),
        "ssd_w_out": nrm((N_ODD, D_INNER, D), D_INNER ** -0.5),
        "moe_router": nrm((N_ODD, D, N_EXPERTS), D ** -0.5),
        "moe_w_gate": nrm((N_ODD, N_EXPERTS, D, D_FF_EXPERT), D ** -0.5),
        "moe_w_up": nrm((N_ODD, N_EXPERTS, D, D_FF_EXPERT), D ** -0.5),
        "moe_w_down": nrm((N_ODD, N_EXPERTS, D_FF_EXPERT, D), D_FF_EXPERT ** -0.5),
        "final_g": gain((D,)),
    }

def reference(x, c, ctx, c_ctx, ada_w, ada_b, norm1_g, norm2_g, ab_w_in, ab_conv_w, ab_sink, ab_w_out,
              ffn_w_gate, ffn_w_up, ffn_w_down, ssd_w_in, ssd_conv_w, ssd_conv_b, ssd_dt_bias_f,
              ssd_dt_bias_b, ssd_a_log_f, ssd_a_log_b, ssd_d, ssd_norm_g, ssd_w_out, moe_router,
              moe_w_gate, moe_w_up, moe_w_down, final_g):
    L = x.shape[1]
    cos, sin = rope2d_tables(L)
    sc_x = jax.nn.silu(c)
    sc_c = jax.nn.silu(c_ctx)
    xc = ctx
    for i in range(DEPTH):
        last = i == DEPTH - 1
        j = i // 2
        m = (sc_x @ ada_w[i] + ada_b[i])[:, None, :]
        mc = sc_c @ ada_w[i] + ada_b[i]
        sh1, sc1, g1, sh2, sc2, g2 = jnp.split(m, 6, axis=-1)
        sh1c, sc1c, g1c, sh2c, sc2c, g2c = jnp.split(mc, 6, axis=-1)
        h = modulate(x, norm1_g[i], sh1, sc1)
        hc = modulate(xc, norm1_g[i], sh1c, sc1c)
        if i % 2 == 0:
            y, yc = mixer_ab(h, hc, ab_w_in[j], ab_conv_w[j], ab_sink[j], ab_w_out[j], cos, sin, last)
            ffn = lambda t, j=j: swiglu(t, ffn_w_gate[j], ffn_w_up[j], ffn_w_down[j])
        else:
            y, yc = mixer_ssd(h, hc, ssd_w_in[j], ssd_conv_w[j], ssd_conv_b[j], ssd_dt_bias_f[j],
                              ssd_dt_bias_b[j], ssd_a_log_f[j], ssd_a_log_b[j], ssd_d[j],
                              ssd_norm_g[j], ssd_w_out[j], last)
            ffn = lambda t, j=j: moe_ffn(t, moe_router[j], moe_w_gate[j], moe_w_up[j], moe_w_down[j])
        x = x + g1 * y
        x = x + g2 * ffn(modulate(x, norm2_g[i], sh2, sc2))
        if not last:
            xc = xc + g1c * yc
            xc = xc + g2c * ffn(modulate(xc, norm2_g[i], sh2c, sc2c))
    return rmsnorm(x, final_g)


_drawn_inputs = setup_inputs


def setup_inputs(seed=0):
    import zlib

    import numpy as np

    out = dict(_drawn_inputs(seed))
    spreads = {}
    factors = {'ctx': 4.332,
     'c_ctx': 9.69,
     'norm1_g': 7.248,
     'norm2_g': 56.289,
     'ab_sink': 8.0,
     'ssd_conv_b': 200.0,
     'ssd_d': 200.0,
     'ssd_norm_g': 200.0,
     'final_g': 24.885,
     'ssd_dt_bias_f': 8.0,
     'ssd_dt_bias_b': 8.0,
     'ssd_a_log_f': 8.0,
     'ssd_a_log_b': 8.0}
    for name, (base, spread) in spreads.items():
        noise = np.random.default_rng([zlib.crc32(name.encode()), seed]).standard_normal(out[name].shape)
        drawn = base * np.exp(spread * noise) if base else spread * noise
        out[name] = __import__('jax').numpy.asarray(drawn.astype(out[name].dtype))
    for name, factor in factors.items():
        out[name] = (out[name] * factor).astype(out[name].dtype)
    return out
```

```python
from contextlib import ExitStack

import numpy as np

import concourse.bass as bass
from concourse import mybir

F32 = mybir.dt.float32
F32R = mybir.dt.float32r
I32 = mybir.dt.int32
ALU = mybir.AluOpType
ACT = mybir.ActivationFunctionType
AX_X = mybir.AxisListType.X

P = 128
D = 1024
KD = D // P
L = 256
LC = 256
T = L + LC
TB = T // P
LB = L // P
GRID_W = 64
EPS = 1e-6
CONV_CH = 512
HD = 64
NQ, NKV = 8, 2
WINDOW = 128
ROPE_PAIRS = HD // 4
DFF = 2816
NF = DFF // P
DI = 2048
SH, SG_, SN, SPD = 32, 4, 128, 64
REP = SH // SG_
DT_OFF = 2 * DI + 2 * SG_ * SN
NE = 8
FE = 3584
NFE = FE // P
NEG = -1.0e30

RING = 7
SLOT = 4096
UNIT = 2048
UNITS = 42
RAWS, PAIRS = 7, 3

SMALL = {}
_c = 0
for _name, _n in (("c", 16), ("ada_b", 96), ("norm_g", 32), ("final_g", 8), ("ab_conv", 12), ("ssd_conv", 72),
                  ("ssd_conv_b", 24), ("ssd_norm_g", 16), ("router", 64), ("sink", 8), ("dt_bias", 64),
                  ("a_log", 64), ("ssd_d", 32)):
    SMALL[_name] = (_c, _n)
    _c += _n
NSMALL = _c

CONST = {}
_c = 0
for _name, _n in (("ident", 128), ("ones", 128), ("le", 128), ("ge", 128), ("lt", 128), ("gt", 128),
                  ("iota", 128), ("rot", 128)):
    CONST[_name] = (_c, _n)
    _c += _n
NCONST = _c
NROPE = 2 * L + LB * T


class Tally:

    def __init__(self, eng, sem, n=0):
        self.eng, self.sem, self.n = eng, sem, n

    def inc(self, ins):
        ins.then_inc(self.sem, 1)
        self.n = self.n + 1

    def step(self, ins):
        self.inc(ins)
        self.eng.wait_ge(self.sem, self.n)


def build(nc, A, out):
    with ExitStack() as ctx:
        arena_byte = -(-nc.sbuf_base // 32) * 32
        arena_n = nc.sbuf_bytes_remaining // 4 // 8 * 8
        arena = ctx.enter_context(nc.sbuf_tensor("arena", [P, arena_n], F32))
        psum = ctx.enter_context(nc.psum_tensor("psum", [P, 8, 512], F32))

        def sem(name):
            return ctx.enter_context(nc.semaphore(name))

        place = {"at": 0}

        def at(off, *dims):
            n = int(np.prod(dims))
            assert off + n <= arena_n, (off, dims, arena_n)
            v = arena[:, off:off + n]
            if len(dims) == 2:
                v = v.rearrange("p (a b) -> p a b", a=dims[0])
            elif len(dims) == 3:
                v = v.rearrange("p (a b c) -> p a b c", a=dims[0], b=dims[1])
            return v

        def take(*dims):
            v = at(place["at"], *dims)
            place["at"] += int(np.prod(dims))
            return v

        def take_r(name, *dims):
            n = int(np.prod(dims))
            place["at"] += (-place["at"]) % 8
            t = nc.alloc_sbuf_tensor_at(name, [P, *dims], F32R, offset=arena_byte + 4 * place["at"])
            place["at"] += n
            assert place["at"] <= arena_n
            return t

        smalls = take(NSMALL)
        consts = take(NCONST)
        XT = take(KD, T)
        place["at"] += (-place["at"]) % 8
        ht_at = place["at"]
        HT = take(KD, T)
        cond = take(KD, 2)
        MOD = take(2, 48, 2)
        GAIN = take(4, KD, 2)
        RSTD = take(T)
        place["at"] += (-place["at"]) % 8
        ring_at = place["at"]
        ring = [at(ring_at + s * SLOT, SLOT) for s in range(RING)]
        area = ring_at + RING * SLOT
        ssd_area = ring_at + 3 * SLOT

        def small(name):
            o, n = SMALL[name]
            return smalls[:, o:o + n]

        def const(name):
            o, n = CONST[name]
            return consts[:, o:o + n]

        ident, ones = const("ident"), const("ones")

        place["at"] = area
        HA = take(4, T)
        CAT = take(8, T)
        Q = take(4, T)
        KK = take(2, T)
        V = take(TB, P)
        SS = HA.rearrange("p a b -> p (a b)")[:, 0:3 * T].rearrange("p (a b) -> p a b", a=3)
        PTS = take(2, T)
        ropec = take(NROPE)
        cosT, sinT = ropec[:, 0:L], ropec[:, L:2 * L]
        smask = ropec[:, 2 * L:].rearrange("p (a b) -> p a b", a=LB)
        rtmp = take(L)
        att_s = take(8, 8)
        place["at"] = area
        AT = take(NF, T)
        GS = take(2, T)
        ROW = take(2, 512)
        place["at"] = ssd_area
        ZS = take(16, L)
        XTOK = take(TB, DI)
        BTOK = take(TB, SG_ * SN)
        BF = take(SG_, T)
        CF = take(SG_, L)
        CV = take(2, T)
        XW = take(6, 512)
        XD = take(4, 512)
        RT = take(2, 512)
        EX = take(2, 512)
        YT = take(2, 512)
        XS = take(512)
        DTT = take(TB, 64)
        DA = take(TB, 64)
        DTMP = take(4, TB * 64)
        NEGA = take(64)
        ACUM = take(12, SH)
        DEC = take(12, SH)
        SW = take(6, SH)
        CBM = take(2, 2, P)
        S = HT.rearrange("p a b -> p (a b)")[:, 0:2048].rearrange("p (a b) -> p a b", a=4)
        MM = HT.rearrange("p a b -> p (a b)")[:, 2048:4096].rearrange("p (a b c) -> p a b c", a=2, b=2)
        SQ2 = XTOK.rearrange("p a b -> p (a b)")[:, 0:16 * L].rearrange("p (a b) -> p a b", a=16)
        place["at"] = ring_at
        raw = [take(UNIT) for _ in range(RAWS)]
        WH = [take_r(f"weight_hi{i}", UNIT) for i in range(PAIRS)]
        WL = [take_r(f"weight_lo{i}", UNIT) for i in range(PAIRS)]
        TOKH, TOKL = take_r("tokens_hi", LB, D), take_r("tokens_lo", LB, D)
        HSH, HSL = take_r("slots_hi", KD, P), take_r("slots_lo", KD, P)
        AEL = take_r("hidden_lo", NFE, P)
        PM = take_r("one_hot", LB, P)
        SIL = take(2, 512)
        AC = take(2, 512)
        YE = take(1024)
        GPT = take(L)
        GP = take(LB, P)
        iota_hi = take(P)
        POS = take(LB, NE + 1)
        ASG = take(LB, NE + 1)
        GATE = take(LB, NE + 1)
        LG = take(LB, NE)
        RSC = take(16, NE)
        CNT = take(NE)
        flag = take(8)
        place["at"] = ht_at
        AEH = take_r("hidden_hi", NFE, P)
        ACC = XT[:, :, L:T]

        small_in, rope_in, x_in = sem("small_in"), sem("rope_in"), sem("x_in")
        ready = [sem(f"slot_ready{s}") for s in range(RING)]
        ada_row, ada_folded = sem("ada_row"), sem("ada_folded")
        cond_ready, ada_done, mod_ready = sem("cond_ready"), sem("ada_done"), sem("mod_ready")
        sq_ready = [sem(f"sq_ready{i}") for i in range(5)]
        ss_ready = [sem(f"ss_ready{i}") for i in range(5)]
        ms_ready = [sem(f"ms_ready{i}") for i in range(5)]
        rms_ready = [sem(f"rms_ready{i}") for i in range(5)]
        hn_ready = [sem(f"hn_ready{i}") for i in range(5)]
        h_ready = [sem(f"h_ready{i}") for i in range(5)]
        dve_step, act_step, pool_step = sem("dve_step"), sem("act_step"), sem("pool_step")
        in_ready, ha_done, gc_done, gb_done, qkv_done = (sem(n) for n in
                                                         ("in_ready", "ha_done", "gc_done", "gb_done", "qkv_done"))
        rot_ready, rope_done, kk_ready = sem("rot_ready"), sem("rope_done"), sem("kk_ready")
        sc_ready, sc_used, nm_ready, exp_ready, pn_ready = (sem(n) for n in
                                                            ("sc_ready", "sc_used", "nm_ready", "exp_ready", "pn_ready"))
        pt_ready, pt_copied, pv_ready, att_out = (sem(n) for n in ("pt_ready", "pt_copied", "pv_ready", "att_out"))
        abo_ready, abo_added = sem("abo_ready"), sem("abo_added")
        gu_ready, gate_done, ff_done = sem("gu_ready"), sem("gate_done"), sem("ff_done")
        dn_ready, dn_added = sem("dn_ready"), sem("dn_added")
        sub_ready, acum_ready = sem("sub_ready"), sem("acum_ready")
        dt_raw, dt_exp_in, dt_exp, a_ready, dec_raw, dec_ready, sw_ready = (
            sem(n) for n in ("dt_raw", "dt_exp_in", "dt_exp", "a_ready", "dec_raw", "dec_ready", "sw_ready"))
        z_ready, z_done = sem("z_ready"), sem("z_done")
        xbc_ready, conv_done, xbc_silu, xtr_ready, xtr_done = (
            sem(n) for n in ("xbc_ready", "conv_done", "xbc_silu", "xtr_ready", "xtr_done"))
        xw_ready, st_ready, s0_done, s1_done, cb_ready, cb_done = (
            sem(n) for n in ("xw_ready", "st_ready", "s0_done", "s1_done", "cb_ready", "cb_done"))
        rt_ready, seg_ready, ex_ready, mm_ready, yo_ready, yd_ready = (
            sem(n) for n in ("rt_ready", "seg_ready", "ex_ready", "mm_ready", "yo_ready", "yd_ready"))
        xs_ready, y_ready, ytr_ready, yz_ready = (sem(n) for n in ("xs_ready", "y_ready", "ytr_ready", "yz_ready"))
        gsq_ready, gss_ready, yn_ready = sem("gsq_ready"), sem("gss_ready"), sem("yn_ready")
        gms_ready, grms_ready = sem("gms_ready"), sem("grms_ready")
        so_ready, so_added = sem("so_ready"), sem("so_added")
        lg_raw, topk_d, topk_e, asg_ready, pos_raw, pos_ready = (
            sem(n) for n in ("lg_raw", "topk_d", "topk_e", "asg_ready", "pos_raw", "pos_ready"))
        htr_ready, htr_done = sem("htr_ready"), sem("htr_done")
        raw_ready = [sem(f"raw_ready{i}") for i in range(RAWS)]
        m_hi, m_lo, m_unit, m_silu, m_act, m_tr, m_trc, m_ael, m_gat, m_hs, m_y, m_sc, m_acc, m_p, m_gp = (
            sem(n) for n in ("m_hi", "m_lo", "m_unit", "m_silu", "m_act", "m_tr", "m_trc", "m_ael", "m_gat", "m_hs",
                             "m_y", "m_sc", "m_acc", "m_p", "m_gp"))
        htl_done = sem("htl_done")
        moe_added, out_ready, out_stored = sem("moe_added"), sem("out_ready"), sem("out_stored")

        block = ctx.enter_context(nc.Block())

        ada_w = [A["ada_w"][l].rearrange("(k p) n -> p k n", p=P) for l in range(2)]
        ab_in = A["ab_w_in"][0].rearrange("(k p) n -> p k n", p=P)
        ab_out = A["ab_w_out"][0].rearrange("(k p) n -> p k n", p=P)
        w_gate = A["ffn_w_gate"][0].rearrange("(k p) n -> p k n", p=P)
        w_up = A["ffn_w_up"][0].rearrange("(k p) n -> p k n", p=P)
        w_down = A["ffn_w_down"][0].rearrange("(k p) n -> p k n", p=P)
        ssd_in = A["ssd_w_in"][0].rearrange("(k p) n -> p k n", p=P)
        ssd_out = A["ssd_w_out"][0].rearrange("(k p) n -> p k n", p=P)
        e_gate = A["moe_w_gate"][0].rearrange("e (k p) n -> e p k n", p=P)
        e_up = A["moe_w_up"][0].rearrange("e (k p) n -> e p k n", p=P)
        e_down = A["moe_w_down"][0].rearrange("e (k p) n -> e p k n", p=P)


        @block.sync
        def _(sp):
            sp.dma_start(smalls, A["smalls"]).then_inc(small_in, 16)
            sp.dma_start(consts, A["consts"]).then_inc(small_in, 16)
            sp.dma_start(XT, A["xT"].rearrange("(k p) t -> p k t", p=P)).then_inc(x_in, 16)
            freed = [None] * RING

            def load(slot, pieces, by):
                if freed[slot] is not None:
                    sp.wait_ge(*freed[slot])
                for dst, src in pieces:
                    sp.dma_start(dst, src).then_inc(ready[slot], 16)
                freed[slot] = by

            def wide(slot, w, c0, n=512):
                v = ring[slot][:, 0:KD * n].rearrange("p (k n) -> p k n", k=KD)
                return [(v[:, 0:4, :], w[:, 0:4, bass.ds(c0, n)]), (v[:, 4:8, :], w[:, 4:8, bass.ds(c0, n)])]

            for c in range(12):
                load(c % 4, wide(c % 4, ada_w[0], c * 512), (ada_done, c + 1))
            load(4, wide(4, ab_in, 2 * CONV_CH), (in_ready, 4))
            load(5, wide(5, ab_in, CONV_CH), (in_ready, 8))
            load(6, wide(6, ab_in, 0), (in_ready, 12))
            load(0, wide(0, ab_in, 3 * CONV_CH), (in_ready, 16))
            load(1, wide(1, ab_in, 3 * CONV_CH + 512, 256), (in_ready, 21))
            sp.dma_start(ropec, A["rope"]).then_inc(rope_in, 16)
            load(2, wide(2, ab_out, 0), (abo_ready, 4))
            load(3, wide(3, ab_out, 512), (abo_ready, 8))

            def gate_up(slot, c0):
                v = ring[slot].rearrange("p (k n) -> p k n", k=KD)
                return [(v[:, :, 0:256], w_gate[:, :, bass.ds(c0, 256)]), (v[:, :, 256:512], w_up[:, :, bass.ds(c0, 256)])]

            load(0, gate_up(0, 0), (gu_ready, 4))
            load(4, wide(4, ada_w[1], 0), (ada_done, 13))
            load(1, gate_up(1, 256), (gu_ready, 8))
            load(5, wide(5, ada_w[1], 512), (ada_done, 14))
            with sp.Fori(1, 5) as i:
                sp.wait_ge(gu_ready, 8 * i - 4)
                for dst, src in gate_up(0, i * 512):
                    sp.dma_start(dst, src).then_inc(ready[0], 16)
                sp.wait_ge(ada_done, 2 * i + 11)
                for dst, src in wide(4, ada_w[1], i * 1024):
                    sp.dma_start(dst, src).then_inc(ready[4], 16)
                sp.wait_ge(gu_ready, 8 * i)
                for dst, src in gate_up(1, i * 512 + 256):
                    sp.dma_start(dst, src).then_inc(ready[1], 16)
                sp.wait_ge(ada_done, 2 * i + 12)
                for dst, src in wide(5, ada_w[1], i * 1024 + 512):
                    sp.dma_start(dst, src).then_inc(ready[5], 16)
            for s, by in ((0, (gu_ready, 36)), (1, (gu_ready, 40)), (4, (ada_done, 21)), (5, (ada_done, 22))):
                freed[s] = by
            load(0, gate_up(0, 2560), (gu_ready, 44))
            load(4, wide(4, ada_w[1], 5120), (ada_done, 23))
            load(5, wide(5, ada_w[1], 5632), (ada_done, 24))

            for j in range(4):
                for half in range(2):
                    s = (1, 2, 3, 6)[(2 * j + half) % 4]
                    v = ring[s][:, 0:11 * 256].rearrange("p (k n) -> p k n", k=11)
                    w = w_down[:, 11 * half:11 * half + 11, 256 * j:256 * j + 256]
                    load(s, [(v[:, 0:6, :], w[:, 0:6, :]), (v[:, 6:11, :], w[:, 6:11, :])],
                         (dn_ready, 3 * j + 1 + 2 * half))
            load(0, wide(0, ssd_in, DT_OFF, 64), (dt_raw, 1))
            for i in range(4):
                load((1 + i) % 3, wide((1 + i) % 3, ssd_in, 512 * i), (z_ready, 4 * i + 4))
            for i in range(6):
                load((5 + i) % 3, wide((5 + i) % 3, ssd_in, DI + 512 * i), (xbc_ready, 4 * i + 4))
            for j in range(4):
                s = (11 + j) % 3
                v = ring[s].rearrange("p (k n) -> p k n", k=16)
                w = ssd_out[:, :, 256 * j:256 * j + 256]
                load(s, [(v[:, 0:8, :], w[:, 0:8, :]), (v[:, 8:16, :], w[:, 8:16, :])], (so_ready, 2 * j + 2))

            def expert_unit(e, u):
                if u < 28:
                    j, w, half = u // 4, (e_gate, e_up)[u // 2 % 2][e], u % 2
                    return (raw[u % RAWS].rearrange("p (k n) -> p k n", k=4),
                            w[:, 4 * half:4 * half + 4, 512 * j:512 * j + 512])
                j = u - 28
                return raw[u % RAWS].rearrange("p (k n) -> p k n", k=2), e_down[e][:, 2 * j:2 * j + 2, :]

            def expert_loads(e, v, first=False):
                for u in range(UNITS):
                    if first and u < RAWS:
                        sp.wait_ge(so_ready, (4, 6, 8, 8)[u // 2])
                    else:
                        sp.wait_ge(m_lo, UNITS * v + u - RAWS + 1)
                    dst, src = expert_unit(e, u)
                    sp.dma_start(dst, src).then_inc(raw_ready[u % RAWS], 16)

            expert_loads(0, 0, first=True)
            with sp.Fori(1, NE) as e:
                expert_loads(e, e)
            sp.wait_ge(pos_ready, 1)
            most = sp.value_load(flag[0:1, 0:1].bitcast(I32), min_val=0, max_val=L)
            with sp.If(most > P):
                with sp.Fori(0, NE) as e:
                    expert_loads(e, e + NE)
            sp.wait_ge(out_ready, 8)
            sp.dma_start(out.rearrange("(k p) t -> p k t", p=P), HT[:, :, 0:L]).then_inc(out_stored, 16)
            sp.wait_ge(out_stored, 16)

        @block.tensor
        def _(pe):
            uses = [0] * RING

            def arrived(slot):
                uses[slot] += 1
                pe.wait_ge(ready[slot], 32 * uses[slot])

            def norm(i, n):
                for k in range(KD):
                    pe.wait_ge(sq_ready[i], k + 1)
                    last = pe.matmul(psum[:, 6, 0:n], ones, HT[:, k, 0:n], start=k == 0, stop=k == KD - 1)
                last.then_inc(ss_ready[i], 1)

            def project(bank, n, w, cols, norm_i=None, t0=0):
                for k in range(KD):
                    if norm_i is not None:
                        pe.wait_ge(h_ready[norm_i], k + 1)
                    last = pe.matmul(psum[:, bank, 0:n], w[:, k, cols:cols + P], HT[:, k, t0:t0 + n],
                                     start=k == 0, stop=k == KD - 1)
                return last

            def wide(slot, n=512, k=KD):
                return ring[slot][:, 0:k * n].rearrange("p (k n) -> p k n", k=k)

            def ada_chunk(slot, c, first=False):
                bank = 4 + slot % 2
                if not first:
                    pe.wait_ge(ada_row, c - 1)
                for k in range(KD):
                    last = pe.matmul(psum[0:2, bank, :], cond[:, k, :], wide(slot)[:, k, :],
                                     start=k == 0, stop=k == KD - 1)
                last.then_inc(ada_done, 1)

            def ada_fold(slot, c):
                pe.wait_ge(ada_row, c + 1)
                for t in range(4):
                    last = pe.matmul(psum[:, 7, bass.ds((4 * c + t) * 2, 2)], ROW[0:2, slot % 2, t * P:(t + 1) * P],
                                     ident[0:2, 0:2], start=True, stop=True)
                last.then_inc(ada_folded, 1)

            pe.wait_ge(small_in, 32)
            norm(0, T)
            pe.wait_ge(cond_ready, 1)
            for c in range(12):
                arrived(c % 4)
                ada_chunk(c % 4, c, first=c < 2)
                if c:
                    ada_fold(c - 1, c - 1)
            ada_fold(11, 11)
            for c, (slot, done) in enumerate(((4, None), (5, ha_done), (6, gc_done), (0, gb_done))):
                arrived(slot)
                for t in range(4):
                    if done is not None:
                        pe.wait_ge(done, t + 1)
                    project(t, T, wide(slot), t * P, 0 if c == 0 else None).then_inc(in_ready, 1)
            arrived(1)
            pe.wait_ge(qkv_done, 1)
            project(0, T, wide(1, 256), 0).then_inc(in_ready, 1)
            for b in range(TB):
                pe.wait_ge(qkv_done, b + 2)
                for k in range(KD):
                    last = pe.matmul(psum[:, (b + 1) % 4, 0:P], HT[:, k, b * P:(b + 1) * P], wide(1, 256)[:, k, P:2 * P],
                                     start=k == 0, stop=k == KD - 1)
                last.then_inc(in_ready, 1)
            for t in range(5):
                pe.wait_ge(qkv_done, t + 1)
                if t >= 2:
                    pe.wait_ge(rope_done, t - 1)
                src = Q[:, t, 0:L] if t < 4 else KK[:, 0, 0:L]
                pe.matmul(psum[:, 4 + t % 2, 0:L], const("rot"), src, start=True, stop=True).then_inc(rot_ready, 1)
            pe.wait_ge(rope_done, 5)
            pe.wait_ge(kk_ready, 1)
            pe.wait_ge(qkv_done, 9)

            for g in range(NKV):
                for s in range(16 + 3):
                    if s < 16:
                        hh, qb = divmod(s, TB)
                        if s >= 2:
                            pe.wait_ge(sc_used, 16 * g + s - 1)
                        lo = (hh % 2) * HD
                        k0 = 0 if qb < LB else L
                        pe.matmul(psum[:, 4 + s % 2, k0:T], Q[lo:lo + HD, 2 * g + hh // 2, qb * P:(qb + 1) * P],
                                  KK[lo:lo + HD, g, k0:T], start=True, stop=True).then_inc(sc_ready, 1)
                    u = s - 2
                    if 0 <= u < 16:
                        qb = u % TB
                        pe.wait_ge(pn_ready, 16 * g + u + 1)
                        if u >= 2:
                            pe.wait_ge(pt_copied, 16 * g + u - 1)
                        for kb in range(0 if qb < LB else LB, TB):
                            last = pe.transpose(psum[:, 6 + u % 2, kb * P:(kb + 1) * P],
                                                SS[:, u % 3, kb * P:(kb + 1) * P], ident)
                        last.then_inc(pt_ready, 1)
                    u = s - 3
                    if u >= 0:
                        hh, qb = divmod(u, TB)
                        lo = (hh % 2) * HD
                        pe.wait_ge(pt_copied, 16 * g + u + 1)
                        if hh % 2 == 0 and qb == 0:
                            pe.wait_ge(att_out, 2 * g)
                        k0 = 0 if qb < LB else LB
                        for kb in range(k0, TB):
                            last = pe.matmul(psum[lo:lo + HD, hh // 2, qb * P:(qb + 1) * P],
                                             V[:, kb, bass.ds(g * HD, HD)], PTS[:, u % 2, kb * P:(kb + 1) * P],
                                             start=kb == k0, stop=kb == TB - 1)
                        last.then_inc(pv_ready, 1)
            pe.wait_ge(gb_done, 4)
            pe.wait_ge(att_out, 4)
            for c in range(2):
                arrived(2 + c)
                for t in range(4):
                    if c:
                        pe.wait_ge(abo_added, t + 1)
                    for k in range(KD):
                        last = pe.matmul(psum[:, t, :], wide(2 + c)[:, k, t * P:(t + 1) * P], CAT[:, k, :],
                                         start=k == 0, stop=k == KD - 1)
                    last.then_inc(abo_ready, 1)
            norm(1, T)

            def gate_up(slot, i):
                for t in range(4):
                    pe.wait_ge(gate_done if t < 2 else ff_done, 2 * i + t % 2)
                    project(t, T, wide(slot), t * P, 1 if t == 0 else None).then_inc(gu_ready, 1)

            pe.wait_ge(abo_added, 8)
            def gate_up_ada(i, first=False):
                for half in range(2):
                    pe.wait_ge(ready[half], 32 * i + 32 * (uses[half] + 1))
                    gate_up(half, 2 * i + half)
                    if not (first and half == 0):
                        ada_fold(4 + half - 1, 12 + 2 * i + half - 1)
                    pe.wait_ge(ready[4 + half], 32 * i + 32 * (uses[4 + half] + 1))
                    ada_chunk(4 + half, 12 + 2 * i + half)

            gate_up_ada(0, first=True)
            with pe.Fori(1, 5) as i:
                gate_up_ada(i)
            for s in (0, 1, 4, 5):
                uses[s] += 5
            arrived(0)
            gate_up(0, 10)
            ada_fold(5, 21)
            arrived(4)
            ada_chunk(4, 22)
            arrived(5)
            ada_chunk(5, 23)
            ada_fold(4, 22)
            ada_fold(5, 23)
            pe.wait_ge(gate_done, 22)
            for j in range(4):
                for half in range(2):
                    slot = (1, 2, 3, 6)[(2 * j + half) % 4]
                    arrived(slot)
                    for t in range(2):
                        if half == 0:
                            if j >= 2:
                                pe.wait_ge(dn_added, 2 * (j - 2) + t + 1)
                            elif j == 0 and t == 0:
                                pe.wait_ge(ff_done, 22)
                        for k in range(11):
                            last = pe.matmul(psum[:, 2 * (j % 2) + t, :], wide(slot, 256, 11)[:, k, t * P:(t + 1) * P],
                                             AT[:, 11 * half + k, :], start=half == 0 and k == 0,
                                             stop=half == 1 and k == 10)
                        if half == 1 or t == 1:
                            last.then_inc(dn_ready, 1)
            norm(2, T)

            arrived(0)
            for b in range(TB):
                for k in range(KD):
                    if b == 0:
                        pe.wait_ge(h_ready[2], k + 1)
                    last = pe.matmul(psum[:, 5, b * 64:(b + 1) * 64], HT[:, k, b * P:(b + 1) * P],
                                     wide(0, 64)[:, k, :], start=k == 0, stop=k == KD - 1)
            last.then_inc(dt_raw, 1)
            pe.wait_ge(dn_added, 8)
            for i in range(4):
                arrived((1 + i) % 3)
                for t in range(4):
                    if i:
                        pe.wait_ge(z_done, 4 * i + t - 3)
                    project(t, L, wide((1 + i) % 3), t * P).then_inc(z_ready, 1)
            pe.wait_ge(a_ready, 1)
            f, b_ = slice(0, SH), slice(SH, 2 * SH)
            for col, terms in enumerate((
                    (("le", 0, f),), (("le", 1, f),), (("ge", 0, b_),), (("ge", 1, b_),),
                    (("ones", 0, f),), (("ones", 1, b_),),
                    (("le", 2, f),), (("ones", 2, f), ("le", 3, f)), (("ones", 3, b_), ("ge", 2, b_)), (("ge", 3, b_),),
                    (("ones", 2, f), ("ones", 3, f)), (("ones", 3, b_), ("ones", 2, b_)))):
                for n, (m, blk, hs) in enumerate(terms):
                    last = pe.matmul(psum[:, 7, col * SH:(col + 1) * SH], const(m), DA[:, blk, hs],
                                     start=n == 0, stop=n == len(terms) - 1)
            last.then_inc(dec_raw, 1)

            def to_tokens(tile):
                pe.wait_ge(xbc_silu, tile + 1)
                if tile >= 2:
                    pe.wait_ge(xtr_done, tile - 1)
                src = CV[:, tile % 2] if tile < 16 else BF[:, tile - 16]
                for b in range(TB):
                    last = pe.transpose(psum[:, (4, 6)[tile % 2], b * P:(b + 1) * P], src[:, b * P:(b + 1) * P], ident)
                last.then_inc(xtr_ready, 1)

            for i in range(6):
                slot = (5 + i) % 3
                arrived(slot)
                for t in range(4):
                    tile = 4 * i + t
                    if i:
                        pe.wait_ge(conv_done, tile - 3)
                    else:
                        pe.wait_ge(z_done, 13 + t)
                    project(t, T if i < 5 else L, wide(slot), t * P).then_inc(xbc_ready, 1)
                    if 1 <= tile <= 20:
                        to_tokens(tile - 1)

            pe.wait_ge(conv_done, 24)
            pe.wait_ge(xtr_done, 20)
            pe.wait_ge(xbc_silu, 24)
            for g in range(SG_):
                for n, (bank, blks) in enumerate(((0, ((2, 2), (3, 3))), (1, ((2, 4), (3, 5))), (2, ((0, 0),)), (3, ((1, 1),)))):
                    for m, (blk, xw) in enumerate(blks):
                        if n == 0 and m == 0:
                            pe.wait_ge(yz_ready, 2 * g)
                        pe.wait_ge(xw_ready, 10 * g + xw + 1)
                        last = pe.matmul(psum[:, bank, :], BTOK[:, blk, bass.ds(g * SN, SN)], XW[:, xw, :],
                                         start=m == 0, stop=m == len(blks) - 1)
                    last.then_inc(st_ready, 1)
                for c in range(LB):
                    last = pe.matmul(psum[:, 4, c * P:(c + 1) * P], BF[:, g, c * P:(c + 1) * P],
                                     CF[:, g, c * P:(c + 1) * P], start=True, stop=True)
                last.then_inc(cb_ready, 1)

                def seg(n):
                    pe.wait_ge(rt_ready, 8 * g + n + 1)
                    if n >= 2:
                        pe.wait_ge(sub_ready, 8 * g + n - 1)
                    pe.matmul(psum[:, 5 + n % 2, :], ones, RT[:, n % 2, :],
                              start=True, stop=True).then_inc(seg_ready, 1)

                def diag(u):
                    c, half = divmod(u, 2)
                    pe.wait_ge(mm_ready, 8 * g + 2 * u + 2)
                    pe.wait_ge(xw_ready, 10 * g + 10)
                    if u == 0:
                        pe.wait_ge(s1_done, 2 * g + 2)
                    for h in range(4):
                        for d in range(2):
                            cols = slice((4 * half + h) * SPD, (4 * half + h + 1) * SPD)
                            last = pe.matmul(psum[:, 2 + c, cols], MM[:, u % 2, d, h * P:(h + 1) * P],
                                             XD[:, 2 * c + d, cols], start=d == 0, stop=d == 1)
                    last.then_inc(yd_ready, 1)

                def off(c):
                    if c == 0:
                        pe.wait_ge(s0_done, 2 * g + 2)
                        pe.wait_ge(s1_done, 2 * g + 2)
                    else:
                        pe.wait_ge(y_ready, 2 * g + 1)
                    for d, state in enumerate(((0, 3), (2, 1))[c]):
                        last = pe.matmul(psum[:, d, :], CF[:, g, c * P:(c + 1) * P], S[:, state, :], start=True, stop=True)
                    last.then_inc(yo_ready, 1)

                def y_back(c):
                    pe.wait_ge(y_ready, 2 * g + c + 1)
                    if c:
                        pe.wait_ge(yz_ready, 2 * g + 1)
                    for t in range(4):
                        last = pe.transpose(psum[:, 7, t * P:(t + 1) * P], YT[:, 0, t * P:(t + 1) * P], ident)
                    last.then_inc(ytr_ready, 1)

                seg(0)
                seg(1)
                off(0)
                for u in range(4):
                    if u < 3:
                        seg(2 * u + 2)
                        seg(2 * u + 3)
                    diag(u)
                    if u == 2:
                        y_back(0)
                        off(1)
                y_back(1)

            pe.wait_ge(yz_ready, 8)
            for g in range(SG_):
                for t in range(4):
                    pe.wait_ge(gsq_ready, 4 * g + t + 1)
                    last = pe.matmul(psum[:, 4 + g % 2, 0:L], ones, SQ2[:, 4 * g + t, :], start=t == 0, stop=t == 3)
                last.then_inc(gss_ready, 1)
                if g in (1, 2):
                    pe.wait_ge(yn_ready, 4 * (g - 1) + 1)
            for j in range(4):
                slot = (11 + j) % 3
                arrived(slot)
                for t in range(2):
                    if j >= 2:
                        pe.wait_ge(so_added, 2 * (j - 2) + t + 1)
                    for k in range(16):
                        pe.wait_ge(yn_ready, k + 1)
                        last = pe.matmul(psum[:, 2 * (j % 2) + t, 0:L], wide(slot, 256, 16)[:, k, t * P:(t + 1) * P],
                                         ZS[:, k, :], start=k == 0, stop=k == 15)
                    last.then_inc(so_ready, 1)
            norm(3, L)

            for b in range(LB):
                for k in range(KD):
                    pe.wait_ge(h_ready[3], k + 1)
                    last = pe.matmul(psum[:, 7, b * NE:(b + 1) * NE], HT[:, k, b * P:(b + 1) * P],
                                     small("router")[:, k * NE:(k + 1) * NE], start=k == 0, stop=k == KD - 1)
            last.then_inc(lg_raw, 1)
            pe.wait_ge(so_added, 8)
            for n in range(4):
                b, half = divmod(n, 2)
                for t in range(4):
                    last = pe.transpose(psum[:, n, t * P:(t + 1) * P], HT[:, 4 * half + t, b * P:(b + 1) * P], ident)
                last.then_inc(htr_ready, 1)
            pe.wait_ge(asg_ready, LB)
            pe.matmul(psum[:, 6, 0:NE], const("lt"), ASG[:, 0, 0:NE], start=True, stop=True)
            pe.matmul(psum[:, 6, NE:2 * NE], ones, ASG[:, 0, 0:NE], start=True, stop=False)
            pe.matmul(psum[:, 6, NE:2 * NE], const("lt"), ASG[:, 1, 0:NE], start=False, stop=True)
            pe.matmul(psum[:, 6, 2 * NE:3 * NE], ones, ASG[:, 0, 0:NE], start=True, stop=False)
            pe.matmul(psum[:, 6, 2 * NE:3 * NE], ones, ASG[:, 1, 0:NE], start=False, stop=True).then_inc(pos_raw, 1)

            def expert(e, v, second, first=False):
                pe.wait_ge(m_p, v + 1 + second)
                if not isinstance(v, int) or v:
                    pe.wait_ge(m_silu, 7 * v)
                    pe.wait_ge(m_act, 7 * v)
                for bank in range(4):
                    for t in range(4):
                        k = 4 * (bank % 2) + t
                        for b in range(LB):
                            last = pe.matmul(psum[:, bank, t * P:(t + 1) * P], (TOKH, TOKL)[bank // 2][:, b, k * P:(k + 1) * P],
                                             PM[:, b, :], start=b == 0, stop=b == LB - 1)
                    last.then_inc(m_gat, 1)
                if not first:
                    scatter(v - 1)

                def to_ff(j):
                    pe.wait_ge(m_act, 7 * v + j + 1)
                    if j >= 2:
                        pe.wait_ge(m_trc, 8 * v + j - 1)
                        pe.wait_ge(m_ael, 7 * v + j - 1)
                    elif j == 0:
                        pe.wait_ge(m_acc, 4 * v + 4)
                    for t in range(4):
                        last = pe.transpose(psum[:, 4 + j % 2, t * P:(t + 1) * P], AC[:, j % 2, t * P:(t + 1) * P], ident)
                    last.then_inc(m_tr, 1)

                def product(bank, xh, xl, wh, wl, start, stop):
                    pe.matmul(psum[:, bank, :], xh, wh, start=start, stop=False)
                    pe.matmul(psum[:, bank, :], xh, wl, start=False, stop=False)
                    return pe.matmul(psum[:, bank, :], xl, wh, start=False, stop=stop)

                pe.wait_ge(m_hs, 4 * v + 4)
                for u in range(UNITS):
                    wh, wl = WH[u % PAIRS], WL[u % PAIRS]
                    if u < 28:
                        j, w, half = u // 4, u // 2 % 2, u % 2
                        if j >= 2 and half == 0:
                            pe.wait_ge((m_silu, m_act)[w], 7 * v + j - 1)
                        pe.wait_ge(m_lo, UNITS * v + u + 1)
                        for k in range(4):
                            cols = slice(k * 512, (k + 1) * 512)
                            last = product(2 * (j % 2) + w, HSH[:, 4 * half + k, :], HSL[:, 4 * half + k, :], wh[:, cols],
                                           wl[:, cols], half == 0 and k == 0, half == 1 and k == 3)
                    else:
                        d = u - 28
                        pe.wait_ge(m_trc, 8 * v + d // 2 + 1)
                        pe.wait_ge(m_ael, 7 * v + d // 2 + 1)
                        pe.wait_ge(m_lo, UNITS * v + u + 1)
                        for t in range(2):
                            for h in range(2):
                                cols = slice(t * 1024 + h * 512, t * 1024 + (h + 1) * 512)
                                last = product(6 + h, AEH[:, 2 * d + t, :], AEL[:, 2 * d + t, :], wh[:, cols], wl[:, cols],
                                               d == 0 and t == 0, d == 13 and t == 1)
                    last.then_inc(m_unit, 1)
                    if u >= 5 and u % 4 == 1 and u <= 29:
                        to_ff((u - 5) // 4)
                    if u == 29:
                        pe.wait_ge(m_gp, v + 1)
                        pe.wait_ge(m_trc, 8 * v + 6)
                        pe.wait_ge(m_ael, 7 * v + 6)
                        for b in range(LB):
                            last = pe.transpose(psum[:, 5, b * P:(b + 1) * P], GP[:, b, :], ident)
                        last.then_inc(m_tr, 1)

            def scatter(v):
                pe.wait_ge(m_trc, 8 * v + 8)
                pe.wait_ge(m_ael, 7 * v + 7)
                pe.wait_ge(m_y, 2 * v + 2)
                for n in range(4):
                    for t in range(2):
                        k = 2 * n + t
                        last = pe.matmul(psum[:, 4 + n, t * L:(t + 1) * L], YE[:, k * P:(k + 1) * P], GPT,
                                         start=True, stop=True)
                    last.then_inc(m_sc, 1)

            pe.wait_ge(htr_done, 4)
            pe.wait_ge(htl_done, 4)
            expert(0, 0, 0, first=True)
            with pe.Fori(1, NE) as e:
                expert(e, e, 0)
            scatter(NE - 1)
            pe.wait_ge(pos_ready, 1)
            most = pe.value_load(flag[0:1, 0:1].bitcast(I32), min_val=0, max_val=L)
            with pe.If(most > P):
                expert(0, NE, 1, first=True)
                with pe.Fori(1, NE) as e:
                    expert(e, e + NE, 1)
                scatter(2 * NE - 1)
            norm(4, L)

        @block.scalar
        def _(act):
            steps = Tally(act, act_step)

            def ada_rows(slot, c, first=False):
                act.wait_ge(ada_done, c + 1)
                if not first:
                    act.wait_ge(ada_folded, c - 1)
                act.activation(ROW[0:2, slot % 2, :], psum[0:2, 4 + slot % 2, :], ACT.Copy).then_inc(ada_row, 1)

            def norm(i, n, ready_sem, value):
                for k in range(KD):
                    act.wait_ge(ready_sem, value(k))
                    act.activation(HT[:, k, 0:n], XT[:, k, 0:n], ACT.Square).then_inc(sq_ready[i], 1)
                act.wait_ge(ms_ready[i], 1)
                act.activation(RSTD[:, 0:n], RSTD[:, 0:n], ACT.Sqrt).then_inc(rms_ready[i], 1)
                if i == 0:
                    for c in range(12):
                        ada_rows(c, c, first=c < 2)
                layer, which = divmod(i, 2)
                if i < 4:
                    act.wait_ge(mod_ready, layer + 1)
                for k in range(KD):
                    act.wait_ge(hn_ready[i], k + 1)
                    if i == 4:
                        act.activation(HT[:, k, 0:n], HT[:, k, 0:n], ACT.Copy, scale=small("final_g")[:, k:k + 1])\
                           .then_inc(out_ready, 1)
                        continue
                    for s in range(n // L):
                        last = act.activation(HT[:, k, s * L:(s + 1) * L], HT[:, k, s * L:(s + 1) * L], ACT.Identity,
                                              scale=GAIN[:, i, k, s:s + 1], bias=MOD[:, layer, 24 * which + k, s:s + 1])
                    last.then_inc(h_ready[i], 1)

            act.wait_ge(small_in, 32)
            act.activation(cond, small("c").rearrange("p (k s) -> p k s", s=2), ACT.Silu).then_inc(cond_ready, 1)
            norm(0, T, x_in, lambda k: 16)
            for t in range(4):
                act.wait_ge(in_ready, t + 1)
                act.activation(HA[:, t, :], psum[:, t, :], ACT.Copy).then_inc(ha_done, 1)
            for t in range(5):
                act.wait_ge(in_ready, 13 + t)
                act.activation(Q[:, t, :] if t < 4 else KK[:, 0, :], psum[:, t % 4, :], ACT.Copy).then_inc(qkv_done, 1)
            for b in range(TB):
                act.wait_ge(in_ready, 18 + b)
                act.activation(V[:, b, :], psum[:, (b + 1) % 4, 0:P], ACT.Copy).then_inc(qkv_done, 1)

            with act.Fori(0, NKV) as g:
                for s in range(16 + 2):
                    if s < 16:
                        hh, qb = divmod(s, TB)
                        k0 = 0 if qb < LB else L
                        act.wait_ge(nm_ready, 16 * g + s + 1)
                        act.activation(SS[:, s % 3, k0:T], SS[:, s % 3, k0:T], ACT.Exp, bias=att_s[:, 1, s % 3:s % 3 + 1],
                                       accum_out=att_s[:, 2, s % 3:s % 3 + 1]).then_inc(exp_ready, 1)
                        act.activation(att_s[:, 3, s % 3:s % 3 + 1], small("sink")[:, bass.ds(4 * g + hh, 1)], ACT.Exp,
                                       bias=att_s[:, 1, s % 3:s % 3 + 1]).then_inc(exp_ready, 1)
                    u = s - 2
                    if u >= 0:
                        hh, qb = divmod(u, TB)
                        k0 = 0 if qb < LB else L
                        act.wait_ge(pt_ready, 16 * g + u + 1)
                        if u >= 2:
                            act.wait_ge(pv_ready, 16 * g + u - 1)
                        act.activation(PTS[:, u % 2, k0:T], psum[:, 6 + u % 2, k0:T], ACT.Copy).then_inc(pt_copied, 1)
                for i in range(2):
                    act.wait_ge(pv_ready, 16 * g + 8 * i + 8)
                    act.activation(CAT[:, 4 + 2 * g + i, :], psum[:, i, :], ACT.Copy).then_inc(att_out, 1)

            norm(1, T, abo_added, lambda k: k + 1)

            def silu_gate(i):
                for t in range(2):
                    act.wait_ge(gu_ready, 4 * i + t + 1)
                    act.wait_ge(ff_done, 2 * i + t)
                    act.activation(GS[:, t, :], psum[:, t, :], ACT.Silu).then_inc(gate_done, 1)

            def gate_and_rows(i):
                for half in range(2):
                    silu_gate(2 * i + half)
                    ada_rows(half, 12 + 2 * i + half)

            gate_and_rows(0)
            with act.Fori(1, 5) as i:
                gate_and_rows(i)
            silu_gate(10)
            ada_rows(0, 22)
            ada_rows(1, 23)
            norm(2, T, dn_added, lambda k: k + 1)

            act.activation(NEGA, small("a_log"), ACT.Exp).then_inc(dt_exp, 1)
            act.wait_ge(dt_exp_in, 1)
            act.activation(DTMP[:, 1, :], DTMP[:, 1, :], ACT.Exp).then_inc(dt_exp, 1)
            for t in range(16):
                act.wait_ge(z_ready, t + 1)
                act.activation(ZS[:, t, :], psum[:, t % 4, 0:L], ACT.Silu).then_inc(z_done, 1)
            act.wait_ge(acum_ready, 1)
            act.activation(DEC, DEC, ACT.Exp).then_inc(dec_ready, 1)

            def token_copy(tile):
                act.wait_ge(xtr_ready, tile + 1)
                dst = XTOK[:, :, tile * P:(tile + 1) * P] if tile < 16 else BTOK[:, :, (tile - 16) * P:(tile - 15) * P]
                act.activation(dst, psum[:, (4, 6)[tile % 2], :].rearrange("p (b c) -> p b c", b=TB), ACT.Copy)\
                   .then_inc(xtr_done, 1)

            for tile in range(24):
                act.wait_ge(conv_done, tile + 1)
                bias = small("ssd_conv_b")[:, tile:tile + 1]
                if tile < 16:
                    dst, n = CV[:, tile % 2], T
                elif tile < 20:
                    dst, n = BF[:, tile - 16], T
                else:
                    dst, n = CF[:, tile - 20], L
                act.activation(dst[:, 0:n], CV[:, tile % 2, 0:n], ACT.Silu, bias=bias).then_inc(xbc_silu, 1)
                if 1 <= tile <= 20:
                    token_copy(tile - 1)

            with act.Fori(0, SG_) as g:
                for i in range(2):
                    act.wait_ge(st_ready, 4 * g + i + 1)
                    act.activation(S[:, i, :], psum[:, i, :], ACT.Copy).then_inc(s0_done, 1)
                for n in range(8):
                    act.wait_ge(sub_ready, 8 * g + n + 1)
                    act.activation(EX[:, n % 2, :], EX[:, n % 2, :], ACT.Exp).then_inc(ex_ready, 1)
            for t in range(16):
                act.wait_ge(yz_ready, 8)
                act.activation(SQ2[:, t, :], ZS[:, t, :], ACT.Square).then_inc(gsq_ready, 1)
            for g in range(SG_):
                act.wait_ge(gms_ready, g + 1)
                act.activation(RSTD[:, 0:L], RSTD[:, 0:L], ACT.Sqrt).then_inc(grms_ready, 1)
            norm(3, L, so_added, lambda k: k + 1)

            for n in range(4):
                b, half = divmod(n, 2)
                act.wait_ge(htr_ready, n + 1)
                act.activation(TOKH[:, b, half * 512:(half + 1) * 512], psum[:, n, :], ACT.Copy).then_inc(htr_done, 1)
            act.wait_ge(topk_d, LB)
            act.activation(RSC[:, 10, 0:LB], RSC[:, 10, 0:LB], ACT.Exp).then_inc(topk_e, 1)

            def results(v):
                act.wait_ge(m_unit, UNITS * v + UNITS)
                for half in range(2):
                    act.activation(YE[:, half * 512:(half + 1) * 512], psum[:, 6 + half, :], ACT.Copy).then_inc(m_y, 1)

            def expert(v, first=False):
                for u in range(UNITS):
                    act.wait_ge(raw_ready[u % RAWS], 16 * (v * (UNITS // RAWS) + u // RAWS + 1))
                    if not first or u >= PAIRS or (not isinstance(v, int) or v):
                        act.wait_ge(m_unit, UNITS * v + u - PAIRS + 1)
                    act.activation(WH[u % PAIRS][:], raw[u % RAWS], ACT.Copy).then_inc(m_hi, 1)
                    if u == 1:
                        if not first:
                            results(v - 1)
                        for n in range(4):
                            act.wait_ge(m_gat, 4 * v + n + 1)
                            act.activation((HSH, HSL)[n // 2][:, 4 * (n % 2):4 * (n % 2) + 4, :],
                                           psum[:, n, :].rearrange("p (a b) -> p a b", a=4), ACT.Copy).then_inc(m_hs, 1)
                    p = u - PAIRS
                    if p >= 0 and p % 4 == 1 and p < 28:
                        j = p // 4
                        act.wait_ge(m_unit, UNITS * v + p + 1)
                        if j >= 2:
                            act.wait_ge(m_act, 7 * v + j - 1)
                        act.activation(SIL[:, j % 2, :], psum[:, 2 * (j % 2), :], ACT.Silu).then_inc(m_silu, 1)
                    if p >= 5 and p % 4 == 1 and p <= 29:
                        j = (p - 5) // 4
                        act.wait_ge(m_tr, 8 * v + j + 1)
                        act.activation(AEH[:, 4 * j:4 * j + 4, :], psum[:, 4 + j % 2, :].rearrange("p (a b) -> p a b", a=4),
                                       ACT.Copy).then_inc(m_trc, 1)
                    if p == 29:
                        act.wait_ge(m_tr, 8 * v + 8)
                        act.activation(GPT, psum[:, 5, 0:L], ACT.Copy).then_inc(m_trc, 1)

            expert(0, first=True)
            with act.Fori(1, NE) as e:
                expert(e)
            results(NE - 1)
            act.wait_ge(pos_ready, 1)
            most = act.value_load(flag[0:1, 0:1].bitcast(I32), min_val=0, max_val=L)
            with act.If(most > P):
                expert(NE, first=True)
                with act.Fori(1, NE) as e:
                    expert(e + NE)
                results(2 * NE - 1)
            norm(4, L, moe_added, lambda k: k + 1)

        @block.gpsimd
        def _(pool):
            pool.wait_ge(sw_ready, 1)
            pool.wait_ge(xtr_done, 16)
            heads = lambda ap: ap.rearrange("p (h d) -> p h d", d=SPD)

            for g in range(SG_):
                for n, (blk, w) in enumerate(((0, None), (1, None), (2, None), (3, None), (2, None), (3, None))):
                    if n == 0:
                        pool.wait_ge(yd_ready, 4 * g)
                    pool.tensor_tensor(heads(XW[:, n, :]), heads(XTOK[:, blk, bass.ds(g * 512, 512)]),
                                       SW[:, n, bass.ds(g * REP, REP)].unsqueeze(2).broadcast_to([P, REP, SPD]),
                                       ALU.mult).then_inc(xw_ready, 1)

                def tri(n):
                    u, d = divmod(n, 2)
                    c, half = divmod(u, 2)
                    if n >= 2:
                        pool.wait_ge(seg_ready, 8 * g + n - 1)
                    pool.tensor_tensor(RT[:, n % 2, :].rearrange("p (h l) -> p h l", h=4),
                                       ident.unsqueeze(1).broadcast_to([P, 4, P]),
                                       ACUM[:, 2 * d + c, bass.ds(g * REP + 4 * half, 4)].unsqueeze(2).broadcast_to([P, 4, P]),
                                       ALU.mult).then_inc(rt_ready, 1)

                tri(0)
                tri(1)
                for n in range(4):
                    c, d = divmod(n, 2)
                    pool.tensor_tensor(heads(XD[:, n, :]), heads(XTOK[:, c, bass.ds(g * 512, 512)]),
                                       DTT[:, c, bass.ds(g * REP + SH * d, REP)].unsqueeze(2).broadcast_to([P, REP, SPD]),
                                       ALU.mult).then_inc(xw_ready, 1)
                for n in range(2, 8):
                    tri(n)
                    if n in (3, 7):
                        c = (n - 3) // 4
                        pool.wait_ge(y_ready, 2 * g + c)
                        pool.tensor_tensor(heads(XS), heads(XTOK[:, c, bass.ds(g * 512, 512)]),
                                           small("ssd_d")[:, bass.ds(g * REP, REP)].unsqueeze(2).broadcast_to([P, REP, SPD]),
                                           ALU.mult).then_inc(xs_ready, 1)

        @block.vector
        def _(dve):
            st = Tally(dve, dve_step)

            def norm(i, n):
                dve.wait_ge(ss_ready[i], 1)
                rs = RSTD[:, 0:n]
                dve.tensor_scalar(rs, psum[:, 6, 0:n], 1.0 / D, EPS, ALU.mult, ALU.add).then_inc(ms_ready[i], 1)
                dve.wait_ge(rms_ready[i], 1)
                st.step(dve.reciprocal(rs, rs))
                for k in range(KD):
                    dve.tensor_tensor(HT[:, k, 0:n], XT[:, k, 0:n], rs, ALU.mult).then_inc(hn_ready[i], 1)

            def modulation(layer):
                dve.wait_ge(ada_folded, 12 * layer + 12)
                bias = small("ada_b")[:, 48 * layer:48 * layer + 48].unsqueeze(2).broadcast_to([P, 48, 2])
                st.step(dve.tensor_tensor(MOD[:, layer], psum[:, 7, 96 * layer:96 * layer + 96]
                                          .rearrange("p (t s) -> p t s", s=2), bias, ALU.add))
                for which in range(2):
                    i = 2 * layer + which
                    gain = small("norm_g")[:, 16 * which + 8 * layer:16 * which + 8 * layer + 8]
                    last = dve.scalar_tensor_tensor(GAIN[:, i], MOD[:, layer, 24 * which + 8:24 * which + 16, :], 1.0,
                                                    gain.unsqueeze(2).broadcast_to([P, KD, 2]), ALU.add, ALU.mult)
                    if which == 0:
                        st.inc(last)
                last.then_inc(mod_ready, 1)
                dve.wait_ge(mod_ready, layer + 1)

            def residual(layer, which, k, src, streams):
                for s in range(streams):
                    cols = slice(s * L, (s + 1) * L)
                    last = dve.scalar_tensor_tensor(XT[:, k, cols], src[:, cols], MOD[:, layer, 24 * which + 16 + k, s:s + 1],
                                                    XT[:, k, cols], ALU.mult, ALU.add)
                return last

            def conv(dst, src, w, n):
                d3 = dst[:, 0:n].rearrange("p (s l) -> p s l", l=L)
                s3 = src[:, 0:n].rearrange("p (s l) -> p s l", l=L)
                st.step(dve.tensor_scalar(d3, s3, w[1], None, ALU.mult))
                st.step(dve.scalar_tensor_tensor(d3[:, :, 1:L], s3[:, :, 0:L - 1], w[0], d3[:, :, 1:L], ALU.mult, ALU.add))
                return dve.scalar_tensor_tensor(d3[:, :, 0:L - 1], s3[:, :, 1:L], w[2], d3[:, :, 0:L - 1],
                                                ALU.mult, ALU.add)

            dve.wait_ge(small_in, 32)
            dve.wait_ge(x_in, 16)
            norm(0, T)
            modulation(0)
            for t in range(4):
                dve.wait_ge(in_ready, 5 + t)
                dve.wait_ge(ha_done, t + 1)
                dve.tensor_tensor(HA[:, t, :], psum[:, t, :], HA[:, t, :], ALU.mult).then_inc(gc_done, 1)
                dve.wait_ge(gc_done, t + 1)
                w = [small("ab_conv")[:, 4 * i + t:4 * i + t + 1] for i in range(3)]
                st.step(conv(CAT[:, t, :], HA[:, t, :], w, T))
            for t in range(4):
                dve.wait_ge(in_ready, 9 + t)
                dve.tensor_tensor(CAT[:, t, :], psum[:, t, :], CAT[:, t, :], ALU.mult).then_inc(gb_done, 1)
            dve.wait_ge(rope_in, 16)
            for t in range(5):
                x = Q[:, t, 0:L] if t < 4 else KK[:, 0, 0:L]
                dve.wait_ge(rot_ready, t + 1)
                if t:
                    dve.wait_ge(rope_done, t)
                st.inc(dve.tensor_tensor(rtmp, psum[:, 4 + t % 2, 0:L], sinT, ALU.mult))
                st.step(dve.tensor_tensor(x, x, cosT, ALU.mult))
                dve.tensor_tensor(x, x, rtmp, ALU.add).then_inc(rope_done, 1)
            dve.wait_ge(rope_done, 5)
            st.inc(dve.tensor_copy(KK[0:HD, 1, :], KK[HD:P, 0, :]))
            st.step(dve.tensor_copy(KK[HD:P, 1, :], KK[HD:P, 0, :]))
            dve.tensor_copy(KK[HD:P, 0, :], KK[0:HD, 0, :]).then_inc(kk_ready, 1)

            steps0 = st.n
            per_g = 16 * 3
            with dve.Fori(0, NKV) as g:
                st.n = steps0 + per_g * g
                for s in range(16 + 1):
                    if s < 16:
                        hh, qb = divmod(s, TB)
                        b = s % 3
                        dve.wait_ge(sc_ready, 16 * g + s + 1)
                        if s >= 3:
                            dve.wait_ge(pt_ready, 16 * g + s - 2)
                        k0 = 0 if qb < LB else L
                        src = psum[:, 4 + s % 2, k0:T]
                        if qb < LB:
                            dve.scalar_tensor_tensor(SS[:, b, :], src, HD ** -0.5, smask[:, qb, :], ALU.mult, ALU.add)\
                               .then_inc(sc_used, 1)
                        else:
                            dve.tensor_scalar(SS[:, b, k0:T], src, HD ** -0.5, None, ALU.mult).then_inc(sc_used, 1)
                        dve.wait_ge(sc_used, 16 * g + s + 1)
                        st.step(dve.reduce_max(att_s[:, 0, b:b + 1], SS[:, b, k0:T], AX_X))
                        dve.tensor_scalar(att_s[:, 1, b:b + 1], att_s[:, 0, b:b + 1],
                                              small("sink")[:, bass.ds(4 * g + hh, 1)], -1.0, ALU.max, ALU.mult)\
                               .then_inc(nm_ready, 1)
                    u = s - 1
                    if u >= 0:
                        b = u % 3
                        k0 = 0 if u % TB < LB else L
                        dve.wait_ge(exp_ready, 32 * g + 2 * u + 2)
                        st.step(dve.tensor_tensor(att_s[:, 4, b:b + 1], att_s[:, 2, b:b + 1], att_s[:, 3, b:b + 1], ALU.add))
                        st.step(dve.reciprocal(att_s[:, 5, b:b + 1], att_s[:, 4, b:b + 1]))
                        dve.tensor_scalar(SS[:, b, k0:T], SS[:, b, k0:T], att_s[:, 5, b:b + 1], None, ALU.mult)\
                           .then_inc(pn_ready, 1)
            st.n = steps0 + per_g * NKV

            for k in range(KD):
                dve.wait_ge(abo_ready, k + 1)
                residual(0, 0, k, psum[:, k % 4, :], 2).then_inc(abo_added, 1)
            norm(1, T)
            def gated_up(i):
                for t in range(2):
                    dve.wait_ge(gu_ready, 4 * i + t + 3)
                    dve.wait_ge(gate_done, 2 * i + t + 1)
                    dve.tensor_tensor(AT[:, 2 * i + t, :], psum[:, 2 + t, :], GS[:, t, :], ALU.mult).then_inc(ff_done, 1)

            gated_up(0)
            with dve.Fori(1, 11) as i:
                gated_up(i)
            modulation(1)
            for k in range(KD):
                dve.wait_ge(dn_ready, 3 * (k // 2) + 2 + k % 2)
                residual(0, 1, k, psum[:, k % 4, :], 2).then_inc(dn_added, 1)
            norm(2, T)

            r, e_, z, z2 = (DTMP[:, i, :] for i in range(4))
            blocks = lambda ap: ap.rearrange("p (b h) -> p b h", b=TB)
            dtf = DTT.rearrange("p b h -> p (b h)")
            daf = DA.rearrange("p b h -> p (b h)")
            dve.wait_ge(dt_raw, 1)
            st.step(dve.tensor_tensor(blocks(r), blocks(psum[:, 5, 0:TB * 64]),
                                      small("dt_bias").unsqueeze(1).broadcast_to([P, TB, 64]), ALU.add))
            dve.scalar_tensor_tensor(e_, r, -1.0, r, ALU.mult, ALU.min).then_inc(dt_exp_in, 1)
            dve.wait_ge(dt_exp, 2)
            st.step(dve.tensor_scalar(z, e_, 2.0, None, ALU.add))
            st.step(dve.reciprocal(z, z))
            st.step(dve.tensor_tensor(z, z, e_, ALU.mult))
            st.step(dve.tensor_tensor(z2, z, z, ALU.mult))
            st.step(dve.tensor_scalar(e_, z2, 1.0 / 15, None, ALU.mult))
            for n in (13, 11, 9, 7, 5, 3):
                st.step(dve.scalar_tensor_tensor(e_, e_, 1.0 / n, z2, ALU.add, ALU.mult))
            st.step(dve.scalar_tensor_tensor(e_, e_, 1.0, z, ALU.add, ALU.mult))
            st.step(dve.tensor_scalar(r, r, 0.0, None, ALU.max))
            st.inc(dve.scalar_tensor_tensor(dtf, e_, 2.0, r, ALU.mult, ALU.add))
            st.step(dve.tensor_scalar(NEGA, NEGA, -1.0, None, ALU.mult))
            dve.tensor_tensor(DA, DTT, NEGA.unsqueeze(1).broadcast_to([P, TB, 64]), ALU.mult).then_inc(a_ready, 1)

            def conv_tile(tile):
                dve.wait_ge(xbc_ready, tile + 1)
                if tile in range(2, 18):
                    dve.wait_ge(xtr_ready, tile - 1)
                elif tile >= 18:
                    dve.wait_ge(xbc_silu, tile - 1)
                w = [small("ssd_conv")[:, 24 * i + tile:24 * i + tile + 1] for i in range(3)]
                conv(CV[:, tile % 2], psum[:, tile % 4, :], w, T if tile < 20 else L).then_inc(conv_done, 1)

            conv_tile(0)
            dve.wait_ge(dec_raw, 1)
            st.step(dve.tensor_copy(ACUM, psum[:, 7, 0:12 * SH].rearrange("p (a b) -> p a b", a=12)))
            st.inc(dve.tensor_copy(DEC[:, 0:4, :], ACUM[:, 0:4, :]))
            st.inc(dve.tensor_copy(DEC[:, 6:8, :], ACUM[:, 4:6, :]))
            for n, (total, own) in enumerate(((4, 0), (5, 3), (10, 6), (10, 7), (11, 8), (11, 9))):
                last = dve.tensor_tensor(DEC[:, (4, 5, 8, 9, 10, 11)[n], :], ACUM[:, total, :], ACUM[:, own, :], ALU.subtract)
                if n < 5:
                    st.inc(last)
            last.then_inc(acum_ready, 1)
            dve.wait_ge(dec_ready, 1)
            for n, (col, blk, h0) in enumerate(((4, 0, 0), (5, 1, SH), (8, 2, 0), (9, 3, 0), (10, 2, SH), (11, 3, SH))):
                last = dve.tensor_tensor(SW[:, n, :], DEC[:, col, :], DTT[:, blk, h0:h0 + SH], ALU.mult)
                if n < 5:
                    st.inc(last)
            last.then_inc(sw_ready, 1)
            for tile in range(1, 24):
                conv_tile(tile)

            heads = lambda ap: ap.rearrange("p (h d) -> p h d", d=SPD)

            def per_head(col, g):
                return DEC[:, col, bass.ds(g * REP, REP)].unsqueeze(2).broadcast_to([P, REP, SPD])

            steps1 = st.n
            with dve.Fori(0, SG_) as g:
                st.n = steps1 + 12 * g
                for i in range(2):
                    dve.wait_ge(s0_done, 2 * g + i + 1)
                    st.step(dve.tensor_tensor(heads(S[:, 2 + i, :]), heads(S[:, i, :]), per_head(6 + i, g), ALU.mult))
                    dve.wait_ge(st_ready, 4 * g + 3 + i)
                    dve.tensor_tensor(S[:, 2 + i, :], S[:, 2 + i, :], psum[:, 2 + i, :], ALU.add).then_inc(s1_done, 1)
                dve.wait_ge(cb_ready, g + 1)
                for d, m in enumerate(("le", "ge")):
                    st.inc(dve.tensor_tensor(CBM[:, :, d, :], psum[:, 4, 0:2 * P].rearrange("p (c l) -> p c l", c=2),
                                             const(m).unsqueeze(1).broadcast_to([P, 2, P]), ALU.mult))
                dve.wait_ge(dve_step, st.n)

                def between(n):
                    u, d = divmod(n, 2)
                    c, half = divmod(u, 2)
                    dve.wait_ge(seg_ready, 8 * g + n + 1)
                    if n >= 2:
                        dve.wait_ge(mm_ready, 8 * g + n - 1)
                    for h in range(4):
                        last = dve.tensor_scalar(EX[:, n % 2, h * P:(h + 1) * P], psum[:, 5 + n % 2, h * P:(h + 1) * P],
                                                 ACUM[:, 2 * d + c, bass.ds(g * REP + 4 * half + h, 1)], 0.0,
                                                 ALU.subtract, ALU.min)
                    last.then_inc(sub_ready, 1)

                def decayed(n):
                    u, d = divmod(n, 2)
                    dve.wait_ge(ex_ready, 8 * g + n + 1)
                    if u >= 2:
                        dve.wait_ge(yd_ready, 4 * g + u - 1)
                    dve.tensor_tensor(MM[:, u % 2, d, :].rearrange("p (h l) -> p h l", h=4),
                                      EX[:, n % 2, :].rearrange("p (h l) -> p h l", h=4),
                                      CBM[:, u // 2, d, :].unsqueeze(1).broadcast_to([P, 4, P]), ALU.mult)\
                       .then_inc(mm_ready, 1)
                    if n < 6:
                        between(n + 2)

                def combine(c):
                    dve.wait_ge(yo_ready, 2 * g + c + 1)
                    if c:
                        dve.wait_ge(ytr_ready, 2 * g + 1)
                    st.inc(dve.tensor_tensor(heads(YT[:, 0, :]), heads(psum[:, 0, :]), per_head(c, g), ALU.mult))
                    st.step(dve.tensor_tensor(heads(YT[:, 1, :]), heads(psum[:, 1, :]), per_head(2 + c, g), ALU.mult))
                    st.step(dve.tensor_tensor(YT[:, 0, :], YT[:, 0, :], YT[:, 1, :], ALU.add))
                    dve.wait_ge(xs_ready, 2 * g + c + 1)
                    st.step(dve.tensor_tensor(YT[:, 0, :], YT[:, 0, :], XS, ALU.add))
                    dve.wait_ge(yd_ready, 4 * g + 2 * c + 2)
                    dve.tensor_tensor(YT[:, 0, :], YT[:, 0, :], psum[:, 2 + c, :], ALU.add).then_inc(y_ready, 1)

                def gated(c):
                    dve.wait_ge(ytr_ready, 2 * g + c + 1)
                    zs = ZS[:, bass.ds(4 * g, 4), c * P:(c + 1) * P]
                    dve.tensor_tensor(zs, psum[:, 7, :].rearrange("p (t l) -> p t l", t=4), zs, ALU.mult)\
                       .then_inc(yz_ready, 1)

                between(0)
                between(1)
                for n in range(5):
                    decayed(n)
                combine(0)
                for n in range(5, 8):
                    decayed(n)
                gated(0)
                combine(1)
                gated(1)
            st.n = steps1 + 12 * SG_

            for g in range(SG_):
                dve.wait_ge(gss_ready, g + 1)
                dve.wait_ge(yn_ready, 4 * g)
                rs = RSTD[:, 0:L]
                dve.tensor_scalar(rs, psum[:, 4 + g % 2, 0:L], 1.0 / 512, EPS, ALU.mult, ALU.add).then_inc(gms_ready, 1)
                dve.wait_ge(grms_ready, g + 1)
                st.step(dve.reciprocal(rs, rs))
                for t in range(4):
                    i = 4 * g + t
                    dve.scalar_tensor_tensor(ZS[:, i, :], ZS[:, i, :], small("ssd_norm_g")[:, i:i + 1], rs,
                                             ALU.mult, ALU.mult).then_inc(yn_ready, 1)
            for k in range(KD):
                dve.wait_ge(so_ready, k + 1)
                residual(1, 0, k, psum[:, k % 4, :], 1).then_inc(so_added, 1)
            norm(3, L)

            for n in range(4):
                b, half = divmod(n, 2)
                cols = slice(half * 512, (half + 1) * 512)
                dve.wait_ge(htr_done, n + 1)
                dve.tensor_tensor(TOKL[:, b, cols], psum[:, n, :], TOKH[:, b, cols].bitcast(F32), ALU.subtract)\
                   .then_inc(htl_done, 1)

            dve.wait_ge(lg_raw, 1)
            st.step(dve.tensor_copy(LG, psum[:, 7, 0:LB * NE].rearrange("p (b e) -> p b e", b=LB)))
            st.inc(dve.memset(ASG, 0.0))
            st.inc(dve.memset(GATE, 0.0))
            st.inc(dve.memset(POS, 0.0))
            for b in range(LB):
                m0, eq, cs, sel0, l2, m1, sel1 = (RSC[:, i, :] for i in (0, 1, 2, 3 + b, 5, 6, 7 + b))
                for m, l, sel in ((m0, LG[:, b, :], sel0), (m1, l2, sel1)):
                    st.step(dve.max(m, l))
                    st.step(dve.tensor_scalar(eq, l, m[:, 0:1], None, ALU.is_equal))
                    st.step(dve.tensor_tensor_scan(cs, ones[:, 0:NE], eq, 0.0, ALU.mult, ALU.add))
                    st.step(dve.scalar_tensor_tensor(sel, cs, 1.0, eq, ALU.is_equal, ALU.mult))
                    if sel is sel0:
                        st.step(dve.scalar_tensor_tensor(l2, sel, -3.0e38, l, ALU.mult, ALU.add))
                last = dve.tensor_tensor(RSC[:, 10, b:b + 1], m1[:, 0:1], m0[:, 0:1], ALU.subtract)
                last.then_inc(topk_d, 1)
                dve.tensor_tensor(ASG[:, b, 0:NE], sel0, sel1, ALU.add).then_inc(asg_ready, 1)
                dve.wait_ge(asg_ready, b + 1)
            st.inc(dve.tensor_scalar(iota_hi, const("iota"), float(P), None, ALU.add))
            for n in range(4):
                dve.memset(ACC[:, 2 * n:2 * n + 2, :], 0.0).then_inc(m_acc, 1)
            dve.wait_ge(topk_e, 1)
            ed, w0, w1 = RSC[:, 10, 0:LB], RSC[:, 9, 0:LB], RSC[:, 11, 0:LB]
            st.step(dve.tensor_scalar(w0, ed, 1.0, None, ALU.add))
            st.step(dve.reciprocal(w0, w0))
            st.step(dve.tensor_tensor(w1, ed, w0, ALU.mult))
            for b in range(LB):
                st.step(dve.tensor_scalar(GATE[:, b, 0:NE], RSC[:, 3 + b, :], w0[:, b:b + 1], None, ALU.mult))
                st.step(dve.scalar_tensor_tensor(GATE[:, b, 0:NE], RSC[:, 7 + b, :], w1[:, b:b + 1], GATE[:, b, 0:NE],
                                                 ALU.mult, ALU.add))
            dve.wait_ge(pos_raw, 1)
            st.inc(dve.tensor_copy(POS[:, :, 0:NE], psum[:, 6, 0:LB * NE].rearrange("p (b e) -> p b e", b=LB)))
            st.step(dve.reduce_max(CNT[:, 0:1], psum[:, 6, 2 * NE:3 * NE], AX_X))
            dve.tensor_copy(flag[:, 0:1].bitcast(I32), CNT[:, 0:1]).then_inc(pos_ready, 1)

            def one_hot(iota, e, gathers):
                if not isinstance(gathers, int) or gathers:
                    dve.wait_ge(m_gat, 4 * gathers)
                for b in range(LB):
                    last = dve.tensor_scalar(PM[:, b, :], iota, POS[:, b, bass.ds(e, 1)], ASG[:, b, bass.ds(e, 1)],
                                             ALU.is_equal, ALU.mult)
                last.then_inc(m_p, 1)

            def add_results(v):
                for n in range(4):
                    dve.wait_ge(m_sc, 4 * v + n + 1)
                    acc = ACC[:, 2 * n:2 * n + 2, :]
                    dve.tensor_tensor(acc, psum[:, 4 + n, :].rearrange("p (a b) -> p a b", a=2), acc, ALU.add)\
                       .then_inc(m_acc, 1)

            def expert(e, v, iota, first=False):
                for u in range(UNITS):
                    dve.wait_ge(m_hi, UNITS * v + u + 1)
                    dve.tensor_tensor(WL[u % PAIRS][:], raw[u % RAWS], WH[u % PAIRS][:].bitcast(F32), ALU.subtract)\
                       .then_inc(m_lo, 1)
                    if u == 2 and not first:
                        dve.wait_ge(m_acc, 4 * v)
                        add_results(v - 1)
                    if u == 9:
                        dve.wait_ge(m_tr, 8 * v)
                        for b in range(LB):
                            last = dve.tensor_scalar(GP[:, b, :], iota, POS[:, b, bass.ds(e, 1)], GATE[:, b, bass.ds(e, 1)],
                                                     ALU.is_equal, ALU.mult)
                        last.then_inc(m_gp, 1)
                    if u == 12:
                        one_hot(iota, e + 1, v + 1)
                    p = u - PAIRS
                    if p >= 0 and p % 4 == 3 and p < 28:
                        j = p // 4
                        dve.wait_ge(m_unit, UNITS * v + p + 1)
                        dve.wait_ge(m_silu, 7 * v + j + 1)
                        if j >= 2:
                            dve.wait_ge(m_tr, 8 * v + j - 1)
                        dve.tensor_tensor(AC[:, j % 2, :], psum[:, 2 * (j % 2) + 1, :], SIL[:, j % 2, :], ALU.mult)\
                           .then_inc(m_act, 1)
                    if p >= 5 and p % 4 == 1 and p <= 29:
                        j = (p - 5) // 4
                        dve.wait_ge(m_trc, 8 * v + j + 1)
                        dve.tensor_tensor(AEL[:, 4 * j:4 * j + 4, :], psum[:, 4 + j % 2, :].rearrange("p (a b) -> p a b", a=4),
                                          AEH[:, 4 * j:4 * j + 4, :].bitcast(F32), ALU.subtract).then_inc(m_ael, 1)

            dve.wait_ge(pos_ready, 1)
            one_hot(const("iota"), 0, 0)
            expert(0, 0, const("iota"), first=True)
            with dve.Fori(1, NE) as e:
                expert(e, e, const("iota"))
            dve.wait_ge(m_acc, 4 * NE)
            add_results(NE - 1)
            most = dve.value_load(flag[0:1, 0:1].bitcast(I32), min_val=0, max_val=L)
            with dve.If(most > P):
                one_hot(iota_hi, 0, NE)
                expert(0, NE, iota_hi, first=True)
                with dve.Fori(1, NE) as e:
                    expert(e, e + NE, iota_hi)
                dve.wait_ge(m_acc, 8 * NE)
                add_results(2 * NE - 1)
                dve.wait_ge(m_acc, 8 * NE + 4)
            dve.wait_ge(m_acc, 4 * NE + 4)
            for k in range(KD):
                residual(1, 1, k, ACC[:, k, :], 1).then_inc(moe_added, 1)
            norm(4, L)


def constants():
    t = np.arange(P)
    c = np.zeros((P, NCONST), np.float32)

    def put(name, m):
        o, n = CONST[name]
        c[:, o:o + n] = m

    put("ident", np.eye(P))
    put("ones", 1.0)
    put("le", t[:, None] <= t[None, :])
    put("ge", t[:, None] >= t[None, :])
    put("lt", t[:, None] < t[None, :])
    put("gt", t[:, None] > t[None, :])
    put("iota", t[None, :])
    rot = np.zeros((P, P), np.float32)
    for f in range(P):
        if f % 32 < ROPE_PAIRS:
            rot[f + ROPE_PAIRS, f] = -1.0
        else:
            rot[f - ROPE_PAIRS, f] = 1.0
    put("rot", rot)
    tok = np.arange(L)
    inv = (np.float32(10000.0) ** (-np.arange(ROPE_PAIRS, dtype=np.float32) / np.float32(ROPE_PAIRS))).astype(np.float32)
    f = np.arange(P) % HD
    where = np.where((f // 32)[:, None] == 0, (tok // GRID_W)[None, :], (tok % GRID_W)[None, :]).astype(np.float32)
    ang = where * inv[f % ROPE_PAIRS][:, None]
    q, k = np.arange(L), np.arange(L)
    mask = np.zeros((L, T), np.float32)
    mask[:, :L] = np.where(np.abs(q[:, None] - k[None, :]) <= WINDOW, 0.0, NEG)
    rope = np.concatenate([np.cos(ang), np.sin(ang), mask[:P], mask[P:]], axis=1).astype(np.float32)
    return c, np.ascontiguousarray(rope)


WEIGHTS = ["ada_w", "ab_w_in", "ab_w_out", "ffn_w_gate", "ffn_w_up", "ffn_w_down", "ssd_w_in", "ssd_w_out",
           "moe_w_gate", "moe_w_up", "moe_w_down"]


def lay_out(inputs):
    g = {k: np.asarray(v) for k, v in inputs.items()}

    def cols(v):
        v = v.reshape(-1, v.shape[-1] // P, P)
        return v.transpose(2, 0, 1).reshape(P, -1)

    def rows(*v):
        v = np.concatenate([x.reshape(-1) for x in v])
        return np.broadcast_to(v, (P, v.size))

    parts = {
        "c": np.stack([g["c"][0].reshape(KD, P).T, g["c_ctx"].reshape(KD, P).T], axis=2).reshape(P, 16),
        "ada_b": cols(g["ada_b"]),
        "norm_g": np.concatenate([cols(g["norm1_g"]), cols(g["norm2_g"])], axis=1),
        "final_g": cols(g["final_g"]),
        "ab_conv": cols(g["ab_conv_w"][0]),
        "ssd_conv": cols(g["ssd_conv_w"][0]),
        "ssd_conv_b": cols(g["ssd_conv_b"]),
        "ssd_norm_g": cols(g["ssd_norm_g"]),
        "router": g["moe_router"][0].reshape(KD, P, NE).transpose(1, 0, 2).reshape(P, -1),
        "sink": rows(g["ab_sink"]),
        "dt_bias": rows(g["ssd_dt_bias_f"], g["ssd_dt_bias_b"]),
        "a_log": rows(g["ssd_a_log_f"], g["ssd_a_log_b"]),
        "ssd_d": rows(g["ssd_d"]),
    }
    arrays = {"smalls": np.ascontiguousarray(np.concatenate([parts[k] for k in SMALL], axis=1))}
    arrays["xT"] = np.ascontiguousarray(np.concatenate([g["x"][0].T, g["ctx"][0].T], axis=1))
    arrays["consts"], arrays["rope"] = constants()
    for k in WEIGHTS:
        arrays[k] = np.ascontiguousarray(g[k])
    return arrays


def kernel(**inputs):
    import concourse.bacc as bacc
    from concourse.bass_utils import run_bass_kernel_spmd

    arrays = lay_out(inputs)
    nc = bacc.Bacc("TRN2", target_bir_lowering=False, num_devices=1)
    aps = {k: nc.dram_tensor(k, v.shape, mybir.dt.from_np(v.dtype), kind="ExternalInput").ap() for k, v in arrays.items()}
    out = nc.dram_tensor("outT", (D, L), F32, kind="ExternalOutput").ap()
    build(nc, aps, out)
    r = run_bass_kernel_spmd(nc, [arrays], core_ids=[0])
    return np.ascontiguousarray(r.results[0]["outT"].T)[None]
```

```python
from contextlib import ExitStack

import numpy as np

import concourse.bass as bass
from concourse import mybir

F32 = mybir.dt.float32
F32R = mybir.dt.float32r
I32 = mybir.dt.int32
ALU = mybir.AluOpType
ACT = mybir.ActivationFunctionType
AX_X = mybir.AxisListType.X

P = 128
D = 1024
KD = D // P
L = 256
LC = 256
T = L + LC
TB = T // P
LB = L // P
GRID_W = 64
EPS = 1e-6
CONV_CH = 512
HD = 64
NQ, NKV = 8, 2
WINDOW = 128
ROPE_PAIRS = HD // 4
DFF = 2816
NF = DFF // P
DI = 2048
SH, SG_, SN, SPD = 32, 4, 128, 64
REP = SH // SG_
DT_OFF = 2 * DI + 2 * SG_ * SN
NE = 8
FE = 3584
NFE = FE // P
NEG = -1.0e30

ADA_SLOTS = 4
ADA_SLOT = 4096
UNIT = 2048
UNITS = 42
RAWS, PAIRS = 7, 3

DOWN_ROWS = ((0, 8), (8, 15), (15, 22))
U_IN, U_OUT, U_GU, U_DOWN, U_DT, U_Z, U_XBC, U_SO, U_END = 0, 9, 13, 35, 47, 48, 56, 68, 76

SMALL = {}
_c = 0
for _name, _n in (("c", 16), ("ada_b", 96), ("norm_g", 32), ("final_g", 8), ("ab_conv", 12), ("ssd_conv", 72),
                  ("ssd_conv_b", 24), ("ssd_norm_g", 16), ("router", 64), ("sink", 8), ("dt_bias", 64),
                  ("a_log", 64), ("ssd_d", 32)):
    SMALL[_name] = (_c, _n)
    _c += _n
NSMALL = _c

CONST = {}
_c = 0
for _name, _n in (("ident", 128), ("ones", 128), ("le", 128), ("ge", 128), ("lt", 128), ("gt", 128),
                  ("iota", 128), ("rot", 128)):
    CONST[_name] = (_c, _n)
    _c += _n
NCONST = _c
NROPE = 2 * L + LB * T


class Tally:

    def __init__(self, eng, sem, n=0):
        self.eng, self.sem, self.n = eng, sem, n

    def inc(self, ins):
        ins.then_inc(self.sem, 1)
        self.n = self.n + 1

    def step(self, ins):
        self.inc(ins)
        self.eng.wait_ge(self.sem, self.n)


def build(nc, A, out):
    with ExitStack() as ctx:
        arena_byte = -(-nc.sbuf_base // 32) * 32
        arena_n = nc.sbuf_bytes_remaining // 4 // 8 * 8
        ctx.enter_context(nc.sbuf_tensor("arena", [P, arena_n], F32))
        psum = ctx.enter_context(nc.psum_tensor("psum", [P, 8, 512], F32))

        def sem(name):
            return ctx.enter_context(nc.semaphore(name))

        place = {"at": 0, "count": 0}

        def at(off, *dims):
            assert off + int(np.prod(dims)) <= arena_n, (off, dims, arena_n)
            place["count"] += 1
            return nc.alloc_sbuf_tensor_at(f"buffer{place['count']}", [P, *dims], F32, offset=arena_byte + 4 * off)[:]

        def take(*dims):
            v = at(place["at"], *dims)
            place["at"] += -(-int(np.prod(dims)) // 8) * 8
            return v

        def take_r(name, *dims):
            n = int(np.prod(dims))
            t = nc.alloc_sbuf_tensor_at(name, [P, *dims], F32R, offset=arena_byte + 4 * place["at"])
            place["at"] += n
            assert place["at"] <= arena_n
            return t

        smalls = take(NSMALL)
        consts = take(NCONST)
        XT = take(KD, T)
        ht_at = place["at"]
        HT = take(KD, T)
        cond = take(KD, 2)
        MOD = take(2, 48, 2)
        GAIN = take(4, KD, 2)
        RSTD = take(T)
        ring_at = place["at"]
        HTL = nc.alloc_sbuf_tensor_at("h_lo", [P, KD, T], F32R, offset=arena_byte + 4 * ht_at)
        hth_at = place["at"]
        HTH = take_r("h_hi", KD, T)
        DRAW = [take(UNIT) for _ in range(2)]
        DWH = [take_r(f"dense_hi{i}", KD, 256) for i in range(2)]
        DWL = [take_r(f"dense_lo{i}", KD, 256) for i in range(2)]
        area = place["at"]
        ada_at = arena_n - ADA_SLOTS * ADA_SLOT
        ada_slot = [at(ada_at + s * ADA_SLOT, ADA_SLOT) for s in range(ADA_SLOTS)]

        def small(name):
            o, n = SMALL[name]
            return smalls[:, o:o + n]

        def const(name):
            o, n = CONST[name]
            return consts[:, o:o + n]

        ident, ones = const("ident"), const("ones")

        place["at"] = area
        HA = take(4, T)
        CV4 = take(4, T)
        CATH, CATL = take_r("mixed_hi", 8, T), take_r("mixed_lo", 8, T)
        Q = take(4, T)
        KK = take(2, T)
        V = take(TB, P)
        SS = HA.rearrange("p a b -> p (a b)")[:, 0:3 * T].rearrange("p (a b) -> p a b", a=3)
        PTS = take(2, T)
        ropec = take(NROPE)
        cosT, sinT = ropec[:, 0:L], ropec[:, L:2 * L]
        smask = ropec[:, 2 * L:].rearrange("p (a b) -> p a b", a=LB)
        rtmp = take(L)
        att_s = take(8, 8)
        ADAP = take(KD, 256)
        attention_end, place["at"] = place["at"], area
        ATH, ATL = take_r("ff_hi", NF, T), take_r("ff_lo", NF, T)
        GS = take(2, T)
        ADAW = take(KD, 256)
        ADAC = take(2, 256)
        assert attention_end <= place["at"] - 2 * UNIT
        assert ada_at >= hth_at + 4096
        ROW = at(area, 2, 512)
        assert area + 1024 <= ada_at
        place["at"] = area
        ZS = take(16, L)
        xtok_at = place["at"]
        XTOK = take(TB, DI)
        BTOK = take(TB, SG_ * SN)
        BF = take(SG_, T)
        CF = take(SG_, L)
        CV = take(2, T)
        XW = at(hth_at, 6, 512)
        XD = take(4, 512)
        RT = take(2, 512)
        EX = at(hth_at + 3072, 2, 512)
        YT = take(2, 512)
        XS = take(512)
        DTT = take(TB, 64)
        DA = take(TB, 64)
        DTMP = take(4, TB * 64)
        NEGA = take(64)
        ACUM = take(12, SH)
        DEC = take(12, SH)
        SW = take(6, SH)
        CBM = take(2, 2, P)
        S = HT.rearrange("p a b -> p (a b)")[:, 0:2048].rearrange("p (a b) -> p a b", a=4)
        MM = HT.rearrange("p a b -> p (a b)")[:, 2048:4096].rearrange("p (a b c) -> p a b c", a=2, b=2)
        SQ2 = HT.rearrange("p a b -> p (a b)").rearrange("p (a b) -> p a b", a=16)
        place["at"] = xtok_at
        YNH, YNL = take_r("y_hi", 16, L), take_r("y_lo", 16, L)
        place["at"] = ring_at
        raw = [take(UNIT) for _ in range(RAWS)]
        WH = [take_r(f"weight_hi{i}", UNIT) for i in range(PAIRS)]
        WL = [take_r(f"weight_lo{i}", UNIT) for i in range(PAIRS)]
        TOKH, TOKL = take_r("tokens_hi", LB, D), take_r("tokens_lo", LB, D)
        HSH, HSL = take_r("slots_hi", KD, P), take_r("slots_lo", KD, P)
        AEL = take_r("hidden_lo", NFE, P)
        PM = take_r("one_hot", LB, P)
        SIL = take(2, 512)
        AC = take(2, 512)
        YE = take(1024)
        GPT = take(L)
        GP = take(LB, P)
        iota_hi = take(P)
        POS = take(LB, NE + 1)
        ASG = take(LB, NE + 1)
        GATE = take(LB, NE + 1)
        LG = take(LB, NE)
        RSC = take(16, NE)
        CNT = take(NE)
        flag = take(8)
        place["at"] = ht_at
        AEH = take_r("hidden_hi", NFE, P)
        ACC = XT[:, :, L:T]

        small_in, rope_in, x_in = sem("small_in"), sem("rope_in"), sem("x_in")
        ready = [sem(f"ada_in{s}") for s in range(ADA_SLOTS)]
        raw_in = [sem(f"dense_in{s}") for s in range(2)]
        hi_done, lo_done, tile_done = sem("hi_done"), sem("lo_done"), sem("tile_done")
        adw_in, adc_ready, adc_folded = sem("adw_in"), sem("adc_ready"), sem("adc_folded")
        hh_ready = [sem(f"hh_ready{i}") for i in range(3)]
        hl_ready = [sem(f"hl_ready{i}") for i in range(3)]
        cat_hi, cat_lo, att_lo = sem("cat_hi"), sem("cat_lo"), sem("att_lo")
        f_ready, fh_done, yf_ready, yh_ready = sem("f_ready"), sem("fh_done"), sem("yf_ready"), sem("yh_ready")
        ada_row, ada_folded = sem("ada_row"), sem("ada_folded")
        cond_ready, ada_done, mod_ready = sem("cond_ready"), sem("ada_done"), sem("mod_ready")
        sq_ready = [sem(f"sq_ready{i}") for i in range(5)]
        ss_ready = [sem(f"ss_ready{i}") for i in range(5)]
        ms_ready = [sem(f"ms_ready{i}") for i in range(5)]
        rms_ready = [sem(f"rms_ready{i}") for i in range(5)]
        hn_ready = [sem(f"hn_ready{i}") for i in range(5)]
        h_ready = [sem(f"h_ready{i}") for i in range(5)]
        dve_step, act_step, pool_step = sem("dve_step"), sem("act_step"), sem("pool_step")
        ha_done, gc_done, gb_done, qkv_done = (sem(n) for n in ("ha_done", "gc_done", "gb_done", "qkv_done"))
        rot_ready, rope_done, kk_ready = sem("rot_ready"), sem("rope_done"), sem("kk_ready")
        sc_ready, sc_used, nm_ready, exp_ready, pn_ready = (sem(n) for n in
                                                            ("sc_ready", "sc_used", "nm_ready", "exp_ready", "pn_ready"))
        pt_ready, pt_copied, pv_ready, att_out = (sem(n) for n in ("pt_ready", "pt_copied", "pv_ready", "att_out"))
        abo_added, dn_added, so_added = sem("abo_added"), sem("dn_added"), sem("so_added")
        gate_done, ff_done = sem("gate_done"), sem("ff_done")
        sub_ready, acum_ready = sem("sub_ready"), sem("acum_ready")
        dt_exp_in, dt_exp, a_ready, dec_raw, dec_ready, sw_ready = (
            sem(n) for n in ("dt_exp_in", "dt_exp", "a_ready", "dec_raw", "dec_ready", "sw_ready"))
        z_done, conv_done, xbc_silu, xtr_ready, xtr_done = (
            sem(n) for n in ("z_done", "conv_done", "xbc_silu", "xtr_ready", "xtr_done"))
        xw_ready, st_ready, s0_done, s1_done, cb_ready = (
            sem(n) for n in ("xw_ready", "st_ready", "s0_done", "s1_done", "cb_ready"))
        rt_ready, seg_ready, ex_ready, mm_ready, yo_ready, yd_ready = (
            sem(n) for n in ("rt_ready", "seg_ready", "ex_ready", "mm_ready", "yo_ready", "yd_ready"))
        xs_ready, y_ready, ytr_ready, yz_ready = (sem(n) for n in ("xs_ready", "y_ready", "ytr_ready", "yz_ready"))
        gsq_ready, gss_ready, yn_ready = sem("gsq_ready"), sem("gss_ready"), sem("yn_ready")
        gms_ready, grms_ready = sem("gms_ready"), sem("grms_ready")
        lg_raw, topk_d, topk_e, asg_ready, pos_raw, pos_ready = (
            sem(n) for n in ("lg_raw", "topk_d", "topk_e", "asg_ready", "pos_raw", "pos_ready"))
        htr_ready, htr_done = sem("htr_ready"), sem("htr_done")
        raw_ready = [sem(f"raw_ready{i}") for i in range(RAWS)]
        m_hi, m_lo, m_unit, m_silu, m_act, m_tr, m_trc, m_ael, m_gat, m_hs, m_y, m_sc, m_acc, m_p, m_gp = (
            sem(n) for n in ("m_hi", "m_lo", "m_unit", "m_silu", "m_act", "m_tr", "m_trc", "m_ael", "m_gat", "m_hs",
                             "m_y", "m_sc", "m_acc", "m_p", "m_gp"))
        htl_done = sem("htl_done")
        moe_added, out_ready, out_stored = sem("moe_added"), sem("out_ready"), sem("out_stored")

        block = ctx.enter_context(nc.Block())

        ada_w = [A["ada_w"][l].rearrange("(k p) n -> p k n", p=P) for l in range(2)]
        ab_in = A["ab_w_in"][0].rearrange("(k p) n -> p k n", p=P)
        ab_out = A["ab_w_out"][0].rearrange("(k p) n -> p k n", p=P)
        w_gate = A["ffn_w_gate"][0].rearrange("(k p) n -> p k n", p=P)
        w_up = A["ffn_w_up"][0].rearrange("(k p) n -> p k n", p=P)
        w_down = A["ffn_w_down"][0].rearrange("(k p) n -> p k n", p=P)
        ssd_in = A["ssd_w_in"][0].rearrange("(k p) n -> p k n", p=P)
        ssd_out = A["ssd_w_out"][0].rearrange("(k p) n -> p k n", p=P)
        e_gate = A["moe_w_gate"][0].rearrange("e (k p) n -> e p k n", p=P)
        e_up = A["moe_w_up"][0].rearrange("e (k p) n -> e p k n", p=P)
        e_down = A["moe_w_down"][0].rearrange("e (k p) n -> e p k n", p=P)


        @block.sync
        def _(sp):
            sp.dma_start(smalls, A["smalls"]).then_inc(small_in, 16)
            sp.dma_start(consts, A["consts"]).then_inc(small_in, 16)
            sp.dma_start(XT, A["xT"].rearrange("(k p) t -> p k t", p=P)).then_inc(x_in, 16)

            def rows(w, c0, n=256):
                return w[:, :, bass.ds(c0, n)]

            def load(n, slot, src, first=False):
                if not first:
                    sp.wait_ge(lo_done, n - 1)
                k, cols = src.shape[1], src.shape[2]
                dst = DRAW[slot][:, 0:k * cols].rearrange("p (k n) -> p k n", k=k)
                sp.dma_start(dst, src).then_inc(raw_in[slot], 16)

            for c in range(12):
                if c >= ADA_SLOTS:
                    sp.wait_ge(ada_done, c - ADA_SLOTS + 1)
                v = ada_slot[c % ADA_SLOTS].rearrange("p (k n) -> p k n", k=KD)
                sp.dma_start(v, ada_w[0][:, :, 512 * c:512 * c + 512]).then_inc(ready[c % ADA_SLOTS], 16)
            starts = [2 * CONV_CH, 2 * CONV_CH + 256, CONV_CH, CONV_CH + 256, 0, 256,
                      3 * CONV_CH, 3 * CONV_CH + 256, 3 * CONV_CH + 512]
            for n, c0 in enumerate(starts):
                load(n, n % 2, rows(ab_in, c0), first=n < 2)
            sp.dma_start(ropec, A["rope"]).then_inc(rope_in, 16)
            for i in range(4):
                load(U_OUT + i, (U_OUT + i) % 2, rows(ab_out, 256 * i))

            def load_gate_up(i):
                load(U_GU + 2 * i, 1, rows(w_gate, i * 256))
                load(U_GU + 2 * i + 1, 0, rows(w_up, i * 256))

            with sp.Fori(0, 11) as i:
                load_gate_up(i)
            for j in range(4):
                for h, (k0, k1) in enumerate(DOWN_ROWS):
                    n = U_DOWN + 3 * j + h
                    load(n, n % 2, w_down[:, k0:k1, 256 * j:256 * j + 256])
            load(U_DT, U_DT % 2, rows(ssd_in, DT_OFF, 64))
            for i in range(8):
                load(U_Z + i, i % 2, rows(ssd_in, 256 * i))
            for i in range(12):
                load(U_XBC + i, i % 2, rows(ssd_in, DI + 256 * i))
            for j in range(4):
                for h in range(2):
                    load(U_SO + 2 * j + h, h, ssd_out[:, 8 * h:8 * h + 8, 256 * j:256 * j + 256])

            def expert_unit(e, u):
                if u < 28:
                    j, w, half = u // 4, (e_gate, e_up)[u // 2 % 2][e], u % 2
                    return (raw[u % RAWS].rearrange("p (k n) -> p k n", k=4),
                            w[:, 4 * half:4 * half + 4, 512 * j:512 * j + 512])
                j = u - 28
                return raw[u % RAWS].rearrange("p (k n) -> p k n", k=2), e_down[e][:, 2 * j:2 * j + 2, :]

            def expert_loads(e, v, first=False):
                for u in range(UNITS):
                    if first and u < RAWS:
                        sp.wait_ge(*((tile_done, 2 * U_SO + 2), (lo_done, U_END), (tile_done, 2 * U_END),
                                     (tile_done, 2 * U_END))[u // 2])
                    else:
                        sp.wait_ge(m_lo, UNITS * v + u - RAWS + 1)
                    dst, src = expert_unit(e, u)
                    sp.dma_start(dst, src).then_inc(raw_ready[u % RAWS], 16)

            expert_loads(0, 0, first=True)
            with sp.Fori(1, NE) as e:
                expert_loads(e, e)
            sp.wait_ge(pos_ready, 1)
            most = sp.value_load(flag[0:1, 0:1].bitcast(I32), min_val=0, max_val=L)
            with sp.If(most > P):
                with sp.Fori(0, NE) as e:
                    expert_loads(e, e + NE)
            sp.wait_ge(out_ready, 8)
            sp.dma_start(out.rearrange("(k p) t -> p k t", p=P), HT[:, :, 0:L]).then_inc(out_stored, 16)
            sp.wait_ge(out_stored, 16)

        @block.tensor
        def _(pe):
            def norm(i, n):
                for k in range(KD):
                    pe.wait_ge(sq_ready[i], k + 1)
                    last = pe.matmul(psum[:, 6, 0:n], ones, HT[:, k, 0:n], start=k == 0, stop=k == KD - 1)
                last.then_inc(ss_ready[i], 1)

            def product(dst, wh, wl, xh, xl, start, stop):
                pe.matmul(dst, wh, xh, start=start, stop=False)
                pe.matmul(dst, wh, xl, start=False, stop=False)
                return pe.matmul(dst, wl, xh, start=False, stop=stop)

            def project(n, slot, banks, width, free, xs=None, norm_i=None, rows=(0, KD), last_row=KD):
                xh, xl = xs or (HTH, HTL)
                pe.wait_ge(lo_done, n + 1)
                for t in range(2):
                    if free[t] is not None:
                        pe.wait_ge(*free[t])
                    for k in range(*rows):
                        if norm_i is not None and t == 0:
                            pe.wait_ge(hl_ready[norm_i], k + 1)
                        kk = k - rows[0]
                        last = product(psum[:, banks[t], 0:width], DWH[slot][:, kk, t * P:(t + 1) * P],
                                       DWL[slot][:, kk, t * P:(t + 1) * P], xh[:, k, 0:width], xl[:, k, 0:width],
                                       k == 0, k == last_row - 1)
                    last.then_inc(tile_done, 1)

            def wide(slot):
                return ada_slot[slot].rearrange("p (k n) -> p k n", k=KD)

            def ada_chunk(slot, c, first=False):
                bank = 4 + slot % 2
                if not first:
                    pe.wait_ge(ada_row, c - 1)
                for k in range(KD):
                    last = pe.matmul(psum[0:2, bank, :], cond[:, k, :], wide(slot)[:, k, :],
                                     start=k == 0, stop=k == KD - 1)
                last.then_inc(ada_done, 1)

            def ada_fold(slot, c):
                pe.wait_ge(ada_row, c + 1)
                for t in range(4):
                    last = pe.matmul(psum[:, 7, bass.ds((4 * c + t) * 2, 2)], ROW[0:2, slot % 2, t * P:(t + 1) * P],
                                     ident[0:2, 0:2], start=True, stop=True)
                last.then_inc(ada_folded, 1)

            pe.wait_ge(small_in, 32)
            norm(0, T)
            pe.wait_ge(cond_ready, 1)
            for c in range(12):
                pe.wait_ge(ready[c % ADA_SLOTS], 16 * (c // ADA_SLOTS + 1))
                ada_chunk(c % 4, c, first=c < 2)
                if c:
                    ada_fold(c - 1, c - 1)
            ada_fold(11, 11)

            def fold_sums(c, streams):
                pe.wait_ge(adc_ready, c + 1)
                for t in range(2):
                    for st_ in range(streams):
                        last = pe.matmul(psum[:, 7, bass.ds((48 + 2 * c + t) * 2 + st_, 1)],
                                         ADAC[:, st_, t * P:(t + 1) * P], ones[:, 0:1], start=True, stop=True)
                last.then_inc(adc_folded, 1)

            for n in range(8):
                done = (None, ha_done, gc_done, gb_done)[n // 2]
                free = [done and (done, 2 * (n % 2) + t + 1) for t in range(2)]
                project(n, n % 2, [2 * (n % 2), 2 * (n % 2) + 1], T, free, norm_i=0 if n == 0 else None)
                if n in (2, 4, 6):
                    fold_sums(n // 2 - 1, 2)
            pe.wait_ge(lo_done, 9)
            pe.wait_ge(qkv_done, 1)
            for k in range(KD):
                last = product(psum[:, 0, :], DWH[0][:, k, 0:P], DWL[0][:, k, 0:P], HTH[:, k, :], HTL[:, k, :],
                               k == 0, k == KD - 1)
            last.then_inc(tile_done, 1)
            pe.wait_ge(qkv_done, 2)
            for b in range(TB):
                cols = slice(b * P, (b + 1) * P)
                for k in range(KD):
                    last = product(psum[:, 1, cols], HTH[:, k, cols], HTL[:, k, cols], DWH[0][:, k, P:2 * P],
                                   DWL[0][:, k, P:2 * P], k == 0, k == KD - 1)
            last.then_inc(tile_done, 1)
            for t in range(5):
                pe.wait_ge(qkv_done, t + 1)
                if t >= 2:
                    pe.wait_ge(rope_done, t - 1)
                src = Q[:, t, 0:L] if t < 4 else KK[:, 0, 0:L]
                pe.matmul(psum[:, 4 + t % 2, 0:L], const("rot"), src, start=True, stop=True).then_inc(rot_ready, 1)
            pe.wait_ge(rope_done, 5)
            pe.wait_ge(kk_ready, 1)
            pe.wait_ge(qkv_done, 6)

            for g in range(NKV):
                for s in range(16 + 3):
                    if s < 16:
                        hh, qb = divmod(s, TB)
                        if s >= 2:
                            pe.wait_ge(sc_used, 16 * g + s - 1)
                        lo = (hh % 2) * HD
                        k0 = 0 if qb < LB else L
                        pe.matmul(psum[:, 4 + s % 2, k0:T], Q[lo:lo + HD, 2 * g + hh // 2, qb * P:(qb + 1) * P],
                                  KK[lo:lo + HD, g, k0:T], start=True, stop=True).then_inc(sc_ready, 1)
                    u = s - 2
                    if 0 <= u < 16:
                        qb = u % TB
                        pe.wait_ge(pn_ready, 16 * g + u + 1)
                        if u >= 2:
                            pe.wait_ge(pt_copied, 16 * g + u - 1)
                        for kb in range(0 if qb < LB else LB, TB):
                            last = pe.transpose(psum[:, (6, 2)[u % 2], kb * P:(kb + 1) * P],
                                                SS[:, u % 3, kb * P:(kb + 1) * P], ident)
                        last.then_inc(pt_ready, 1)
                    u = s - 3
                    if u >= 0:
                        hh, qb = divmod(u, TB)
                        lo = (hh % 2) * HD
                        pe.wait_ge(pt_copied, 16 * g + u + 1)
                        if hh % 2 == 0 and qb == 0:
                            pe.wait_ge(att_lo, 2 * g)
                        k0 = 0 if qb < LB else LB
                        for kb in range(k0, TB):
                            last = pe.matmul(psum[lo:lo + HD, hh // 2, qb * P:(qb + 1) * P],
                                             V[:, kb, bass.ds(g * HD, HD)], PTS[:, u % 2, kb * P:(kb + 1) * P],
                                             start=kb == k0, stop=kb == TB - 1)
                        last.then_inc(pv_ready, 1)
                fold_sums(3 + g, 2)
            pe.wait_ge(cat_lo, 4)
            pe.wait_ge(att_lo, 4)
            for i in range(4):
                n = U_OUT + i
                free = [(abo_added, 2 * i + t - 3) if i >= 2 else None for t in range(2)]
                project(n, n % 2, [(2 * n) % 4, (2 * n) % 4 + 1], T, free, xs=(CATH, CATL))
                if i in (1, 3):
                    fold_sums(5 + i // 2, 2)
            norm(1, T)

            def gate_up(i, first=False):
                for w in range(2):
                    done = (gate_done, f_ready)[w]
                    free = [None if first else (done, 2 * i + t - 1) for t in range(2)]
                    project(U_GU + 2 * i + w, 1 - w, ((2, 3), (0, 1))[w], T, free, norm_i=1 if first and w == 0 else None)
                fold_sums(7 + i, 2 if first else 1)

            pe.wait_ge(abo_added, 8)
            gate_up(0, first=True)
            with pe.Fori(1, 11) as i:
                gate_up(i)
            pe.wait_ge(gate_done, 22)
            pe.wait_ge(ff_done, 22)
            for j in range(4):
                for h, rows in enumerate(DOWN_ROWS):
                    n = U_DOWN + 3 * j + h
                    free = [(dn_added, 2 * (j - 2) + t + 1) if h == 0 and j >= 2 else None for t in range(2)]
                    project(n, n % 2, (2 * (j % 2), 2 * (j % 2) + 1), T, free, xs=(ATH, ATL), rows=rows, last_row=NF)
                    if n % 2 == U_DOWN % 2:
                        fold_sums(18 + (n - U_DOWN) // 2, 1)
            norm(2, T)

            pe.wait_ge(lo_done, U_DT + 1)
            s_ = U_DT % 2
            dth, dtl = (w[s_][:].rearrange("p k n -> p (k n)")[:, 0:512].rearrange("p (k n) -> p k n", k=KD)
                        for w in (DWH, DWL))
            for b in range(TB):
                cols = slice(b * P, (b + 1) * P)
                for k in range(KD):
                    if b == 0:
                        pe.wait_ge(hl_ready[2], k + 1)
                    last = product(psum[:, 5, b * 64:(b + 1) * 64], HTH[:, k, cols], HTL[:, k, cols], dth[:, k, :],
                                   dtl[:, k, :], k == 0, k == KD - 1)
                if b % 2:
                    last.then_inc(tile_done, 1)
            pe.wait_ge(dn_added, 8)
            for i in range(8):
                free = [(z_done, 2 * i + t - 3) if i >= 2 else None for t in range(2)]
                project(U_Z + i, i % 2, (2 * (i % 2), 2 * (i % 2) + 1), L, free)
            pe.wait_ge(a_ready, 1)
            f, b_ = slice(0, SH), slice(SH, 2 * SH)
            for col, terms in enumerate((
                    (("le", 0, f),), (("le", 1, f),), (("ge", 0, b_),), (("ge", 1, b_),),
                    (("ones", 0, f),), (("ones", 1, b_),),
                    (("le", 2, f),), (("ones", 2, f), ("le", 3, f)), (("ones", 3, b_), ("ge", 2, b_)), (("ge", 3, b_),),
                    (("ones", 2, f), ("ones", 3, f)), (("ones", 3, b_), ("ones", 2, b_)))):
                for n, (m, blk, hs) in enumerate(terms):
                    last = pe.matmul(psum[:, 7, col * SH:(col + 1) * SH], const(m), DA[:, blk, hs],
                                     start=n == 0, stop=n == len(terms) - 1)
            last.then_inc(dec_raw, 1)

            def to_tokens(tile):
                pe.wait_ge(xbc_silu, tile + 1)
                if tile >= 2:
                    pe.wait_ge(xtr_done, tile - 1)
                src = CV[:, tile % 2] if tile < 16 else BF[:, tile - 16]
                for b in range(TB):
                    last = pe.transpose(psum[:, (4, 6)[tile % 2], b * P:(b + 1) * P], src[:, b * P:(b + 1) * P], ident)
                last.then_inc(xtr_ready, 1)

            for i in range(12):
                free = [(conv_done, 2 * i + t - 3) if i >= 2 else (z_done, 13 + 2 * i + t) for t in range(2)]
                project(U_XBC + i, i % 2, (2 * (i % 2), 2 * (i % 2) + 1), T if i < 10 else L, free)
                for tile in (2 * i - 2, 2 * i - 1):
                    if 0 <= tile < 20:
                        to_tokens(tile)

            pe.wait_ge(conv_done, 24)
            pe.wait_ge(xtr_done, 20)
            pe.wait_ge(xbc_silu, 24)
            for g in range(SG_):
                for n, (bank, blks) in enumerate(((0, ((2, 2), (3, 3))), (1, ((2, 4), (3, 5))), (2, ((0, 0),)), (3, ((1, 1),)))):
                    for m, (blk, xw) in enumerate(blks):
                        if n == 0 and m == 0:
                            pe.wait_ge(yz_ready, 2 * g)
                        pe.wait_ge(xw_ready, 10 * g + xw + 1)
                        last = pe.matmul(psum[:, bank, :], BTOK[:, blk, bass.ds(g * SN, SN)], XW[:, xw, :],
                                         start=m == 0, stop=m == len(blks) - 1)
                    last.then_inc(st_ready, 1)
                for c in range(LB):
                    last = pe.matmul(psum[:, 4, c * P:(c + 1) * P], BF[:, g, c * P:(c + 1) * P],
                                     CF[:, g, c * P:(c + 1) * P], start=True, stop=True)
                last.then_inc(cb_ready, 1)

                def seg(n):
                    pe.wait_ge(rt_ready, 8 * g + n + 1)
                    if n >= 2:
                        pe.wait_ge(sub_ready, 8 * g + n - 1)
                    pe.matmul(psum[:, 5 + n % 2, :], ones, RT[:, n % 2, :],
                              start=True, stop=True).then_inc(seg_ready, 1)

                def diag(u):
                    c, half = divmod(u, 2)
                    pe.wait_ge(mm_ready, 8 * g + 2 * u + 2)
                    pe.wait_ge(xw_ready, 10 * g + 10)
                    if u == 0:
                        pe.wait_ge(s1_done, 2 * g + 2)
                    for h in range(4):
                        for d in range(2):
                            cols = slice((4 * half + h) * SPD, (4 * half + h + 1) * SPD)
                            last = pe.matmul(psum[:, 2 + c, cols], MM[:, u % 2, d, h * P:(h + 1) * P],
                                             XD[:, 2 * c + d, cols], start=d == 0, stop=d == 1)
                    last.then_inc(yd_ready, 1)

                def off(c):
                    if c == 0:
                        pe.wait_ge(s0_done, 2 * g + 2)
                        pe.wait_ge(s1_done, 2 * g + 2)
                    else:
                        pe.wait_ge(y_ready, 2 * g + 1)
                    for d, state in enumerate(((0, 3), (2, 1))[c]):
                        last = pe.matmul(psum[:, d, :], CF[:, g, c * P:(c + 1) * P], S[:, state, :], start=True, stop=True)
                    last.then_inc(yo_ready, 1)

                def y_back(c):
                    pe.wait_ge(y_ready, 2 * g + c + 1)
                    if c:
                        pe.wait_ge(yz_ready, 2 * g + 1)
                    for t in range(4):
                        last = pe.transpose(psum[:, 7, t * P:(t + 1) * P], YT[:, 0, t * P:(t + 1) * P], ident)
                    last.then_inc(ytr_ready, 1)

                seg(0)
                seg(1)
                off(0)
                for u in range(4):
                    if u < 3:
                        seg(2 * u + 2)
                        seg(2 * u + 3)
                    diag(u)
                    if u == 2:
                        y_back(0)
                        off(1)
                y_back(1)

            pe.wait_ge(yz_ready, 8)
            for g in range(SG_):
                for t in range(4):
                    pe.wait_ge(gsq_ready, 4 * g + t + 1)
                    last = pe.matmul(psum[:, 4 + g % 2, 0:L], ones, SQ2[:, 4 * g + t, :], start=t == 0, stop=t == 3)
                last.then_inc(gss_ready, 1)
                if g in (1, 2):
                    pe.wait_ge(gms_ready, g)
            for j in range(4):
                for h in range(2):
                    if j == 0:
                        pe.wait_ge(yn_ready, 8 * h + 8)
                    free = [(so_added, 2 * (j - 2) + t + 1) if h == 0 and j >= 2 else None for t in range(2)]
                    project(U_SO + 2 * j + h, h, (2 * (j % 2), 2 * (j % 2) + 1), L, free, xs=(YNH, YNL),
                            rows=(8 * h, 8 * h + 8), last_row=16)
            norm(3, L)

            for b in range(LB):
                for k in range(KD):
                    pe.wait_ge(h_ready[3], k + 1)
                    last = pe.matmul(psum[:, 7, b * NE:(b + 1) * NE], HT[:, k, b * P:(b + 1) * P],
                                     small("router")[:, k * NE:(k + 1) * NE], start=k == 0, stop=k == KD - 1)
            last.then_inc(lg_raw, 1)
            pe.wait_ge(so_added, 8)
            for n in range(4):
                b, half = divmod(n, 2)
                for t in range(4):
                    last = pe.transpose(psum[:, n, t * P:(t + 1) * P], HT[:, 4 * half + t, b * P:(b + 1) * P], ident)
                last.then_inc(htr_ready, 1)
            pe.wait_ge(asg_ready, LB)
            pe.matmul(psum[:, 6, 0:NE], const("lt"), ASG[:, 0, 0:NE], start=True, stop=True)
            pe.matmul(psum[:, 6, NE:2 * NE], ones, ASG[:, 0, 0:NE], start=True, stop=False)
            pe.matmul(psum[:, 6, NE:2 * NE], const("lt"), ASG[:, 1, 0:NE], start=False, stop=True)
            pe.matmul(psum[:, 6, 2 * NE:3 * NE], ones, ASG[:, 0, 0:NE], start=True, stop=False)
            pe.matmul(psum[:, 6, 2 * NE:3 * NE], ones, ASG[:, 1, 0:NE], start=False, stop=True).then_inc(pos_raw, 1)

            def expert(e, v, second, first=False):
                pe.wait_ge(m_p, v + 1 + second)
                if not isinstance(v, int) or v:
                    pe.wait_ge(m_silu, 7 * v)
                    pe.wait_ge(m_act, 7 * v)
                for bank in range(4):
                    for t in range(4):
                        k = 4 * (bank % 2) + t
                        for b in range(LB):
                            last = pe.matmul(psum[:, bank, t * P:(t + 1) * P], (TOKH, TOKL)[bank // 2][:, b, k * P:(k + 1) * P],
                                             PM[:, b, :], start=b == 0, stop=b == LB - 1)
                    last.then_inc(m_gat, 1)
                if not first:
                    scatter(v - 1)

                def to_ff(j):
                    pe.wait_ge(m_act, 7 * v + j + 1)
                    if j >= 2:
                        pe.wait_ge(m_trc, 8 * v + j - 1)
                        pe.wait_ge(m_ael, 7 * v + j - 1)
                    elif j == 0:
                        pe.wait_ge(m_acc, 4 * v + 4)
                    for t in range(4):
                        last = pe.transpose(psum[:, 4 + j % 2, t * P:(t + 1) * P], AC[:, j % 2, t * P:(t + 1) * P], ident)
                    last.then_inc(m_tr, 1)

                pe.wait_ge(m_hs, 4 * v + 4)
                for u in range(UNITS):
                    wh, wl = WH[u % PAIRS], WL[u % PAIRS]
                    if u < 28:
                        j, w, half = u // 4, u // 2 % 2, u % 2
                        if j >= 2 and half == 0:
                            pe.wait_ge((m_silu, m_act)[w], 7 * v + j - 1)
                        pe.wait_ge(m_lo, UNITS * v + u + 1)
                        for k in range(4):
                            cols = slice(k * 512, (k + 1) * 512)
                            last = product(psum[:, 2 * (j % 2) + w, :], HSH[:, 4 * half + k, :], HSL[:, 4 * half + k, :],
                                           wh[:, cols], wl[:, cols], half == 0 and k == 0, half == 1 and k == 3)
                    else:
                        d = u - 28
                        pe.wait_ge(m_trc, 8 * v + d // 2 + 1)
                        pe.wait_ge(m_ael, 7 * v + d // 2 + 1)
                        pe.wait_ge(m_lo, UNITS * v + u + 1)
                        for t in range(2):
                            for h in range(2):
                                cols = slice(t * 1024 + h * 512, t * 1024 + (h + 1) * 512)
                                last = product(psum[:, 6 + h, :], AEH[:, 2 * d + t, :], AEL[:, 2 * d + t, :], wh[:, cols], wl[:, cols],
                                               d == 0 and t == 0, d == 13 and t == 1)
                    last.then_inc(m_unit, 1)
                    if u >= 5 and u % 4 == 1 and u <= 29:
                        to_ff((u - 5) // 4)
                    if u == 29:
                        pe.wait_ge(m_gp, v + 1)
                        pe.wait_ge(m_trc, 8 * v + 6)
                        pe.wait_ge(m_ael, 7 * v + 6)
                        for b in range(LB):
                            last = pe.transpose(psum[:, 5, b * P:(b + 1) * P], GP[:, b, :], ident)
                        last.then_inc(m_tr, 1)

            def scatter(v):
                pe.wait_ge(m_trc, 8 * v + 8)
                pe.wait_ge(m_ael, 7 * v + 7)
                pe.wait_ge(m_y, 2 * v + 2)
                for n in range(4):
                    for t in range(2):
                        k = 2 * n + t
                        last = pe.matmul(psum[:, 4 + n, t * L:(t + 1) * L], YE[:, k * P:(k + 1) * P], GPT,
                                         start=True, stop=True)
                    last.then_inc(m_sc, 1)

            pe.wait_ge(htr_done, 4)
            pe.wait_ge(htl_done, 4)
            expert(0, 0, 0, first=True)
            with pe.Fori(1, NE) as e:
                expert(e, e, 0)
            scatter(NE - 1)
            pe.wait_ge(pos_ready, 1)
            most = pe.value_load(flag[0:1, 0:1].bitcast(I32), min_val=0, max_val=L)
            with pe.If(most > P):
                expert(0, NE, 1, first=True)
                with pe.Fori(1, NE) as e:
                    expert(e, e + NE, 1)
                scatter(2 * NE - 1)
            norm(4, L)

        @block.scalar
        def _(act):
            steps = Tally(act, act_step)

            def ada_rows(slot, c, first=False):
                act.wait_ge(ada_done, c + 1)
                if not first:
                    act.wait_ge(ada_folded, c - 1)
                act.activation(ROW[0:2, slot % 2, :], psum[0:2, 4 + slot % 2, :], ACT.Copy).then_inc(ada_row, 1)

            def norm(i, n, ready_sem, value):
                for k in range(KD):
                    act.wait_ge(ready_sem, value(k))
                    act.activation(HT[:, k, 0:n], XT[:, k, 0:n], ACT.Square).then_inc(sq_ready[i], 1)
                act.wait_ge(ms_ready[i], 1)
                act.activation(RSTD[:, 0:n], RSTD[:, 0:n], ACT.Sqrt).then_inc(rms_ready[i], 1)
                if i == 0:
                    for c in range(12):
                        ada_rows(c, c, first=c < 2)
                layer, which = divmod(i, 2)
                if i < 4:
                    act.wait_ge(mod_ready, layer + 1)
                def high(k):
                    act.wait_ge(h_ready[i], k + 1)
                    act.activation(HTH[:, k, :], HT[:, k, :], ACT.Copy).then_inc(hh_ready[i], 1)

                for k in range(KD):
                    act.wait_ge(hn_ready[i], k + 1)
                    if i == 4:
                        act.activation(HT[:, k, 0:n], HT[:, k, 0:n], ACT.Copy, scale=small("final_g")[:, k:k + 1])\
                           .then_inc(out_ready, 1)
                        continue
                    for s in range(n // L):
                        last = act.activation(HT[:, k, s * L:(s + 1) * L], HT[:, k, s * L:(s + 1) * L], ACT.Identity,
                                              scale=GAIN[:, i, k, s:s + 1], bias=MOD[:, layer, 24 * which + k, s:s + 1])
                    last.then_inc(h_ready[i], 1)
                    if i < 3 and k:
                        high(k - 1)
                if i < 3:
                    high(KD - 1)

            def split(q, r, first=False):
                act.wait_ge(raw_in[r], 16 * (q + 1))
                if not first:
                    act.wait_ge(tile_done, 4 * q + 2 * r - 2)
                act.activation(DWH[r][:].rearrange("p k n -> p (k n)"), DRAW[r], ACT.Copy).then_inc(hi_done, 1)

            def ahead(n):
                if n + 2 < U_END:
                    split((n + 2) // 2, n % 2)

            act.wait_ge(small_in, 32)
            act.activation(cond, small("c").rearrange("p (k s) -> p k s", s=2), ACT.Silu).then_inc(cond_ready, 1)
            norm(0, T, x_in, lambda k: 16)
            split(0, 0, first=True)
            split(0, 1, first=True)
            for n in range(9):
                for t in range(2):
                    tile = 2 * n + t
                    if tile < 4 or tile >= 12:
                        act.wait_ge(tile_done, tile + 1)
                        if tile < 4:
                            act.activation(HA[:, tile, :], psum[:, tile, :], ACT.Copy).then_inc(ha_done, 1)
                        elif tile < 16:
                            act.activation(Q[:, tile - 12, :], psum[:, tile % 4, :], ACT.Copy).then_inc(qkv_done, 1)
                        elif tile == 16:
                            act.activation(KK[:, 0, :], psum[:, 0, :], ACT.Copy).then_inc(qkv_done, 1)
                        else:
                            act.activation(V, psum[:, 1, :].rearrange("p (b d) -> p b d", b=TB), ACT.Copy)\
                               .then_inc(qkv_done, 1)
                    if t == 0:
                        ahead(n)
            for t in range(4):
                act.wait_ge(gb_done, t + 1)
                act.activation(CATH[:, t, :], CV4[:, t, :], ACT.Copy).then_inc(cat_hi, 1)

            with act.Fori(0, NKV) as g:
                for s in range(16 + 2):
                    if s < 16:
                        hh, qb = divmod(s, TB)
                        k0 = 0 if qb < LB else L
                        act.wait_ge(nm_ready, 16 * g + s + 1)
                        act.activation(SS[:, s % 3, k0:T], SS[:, s % 3, k0:T], ACT.Exp, bias=att_s[:, 1, s % 3:s % 3 + 1],
                                       accum_out=att_s[:, 2, s % 3:s % 3 + 1]).then_inc(exp_ready, 1)
                        act.activation(att_s[:, 3, s % 3:s % 3 + 1], small("sink")[:, bass.ds(4 * g + hh, 1)], ACT.Exp,
                                       bias=att_s[:, 1, s % 3:s % 3 + 1]).then_inc(exp_ready, 1)
                    u = s - 2
                    if u >= 0:
                        hh, qb = divmod(u, TB)
                        k0 = 0 if qb < LB else L
                        act.wait_ge(pt_ready, 16 * g + u + 1)
                        if u >= 2:
                            act.wait_ge(pv_ready, 16 * g + u - 1)
                        act.activation(PTS[:, u % 2, k0:T], psum[:, (6, 2)[u % 2], k0:T], ACT.Copy).then_inc(pt_copied, 1)
                for i in range(2):
                    act.wait_ge(pv_ready, 16 * g + 8 * i + 8)
                    act.activation(CATH[:, 4 + 2 * g + i, :], psum[:, i, :], ACT.Copy).then_inc(att_out, 1)

            for n in range(U_OUT, U_GU):
                ahead(n)
            norm(1, T, abo_added, lambda k: k + 1)

            def gate(i, first=False):
                for t in range(2):
                    act.wait_ge(tile_done, 2 * U_GU + 4 * i + t + 1)
                    if not first:
                        act.wait_ge(ff_done, 2 * i + t - 1)
                    act.activation(GS[:, t, :], psum[:, 2 + t, :], ACT.Silu).then_inc(gate_done, 1)
                    if t == 0:
                        split(i + U_GU // 2 + 1, 1)
                split(i + U_GU // 2 + 2, 0)
                for t in range(2):
                    act.wait_ge(f_ready, 2 * i + t + 1)
                    act.activation(ATH[:, 2 * i + t, :], GS[:, t, :], ACT.Copy).then_inc(fh_done, 1)

            gate(0, first=True)
            with act.Fori(1, 11) as i:
                gate(i)
            for n in range(U_DOWN, U_DT):
                ahead(n)
            norm(2, T, dn_added, lambda k: k + 1)

            act.activation(NEGA, small("a_log"), ACT.Exp).then_inc(dt_exp, 1)
            ahead(U_DT)
            act.wait_ge(dt_exp_in, 1)
            act.activation(DTMP[:, 1, :], DTMP[:, 1, :], ACT.Exp).then_inc(dt_exp, 1)
            for t in range(16):
                act.wait_ge(tile_done, 2 * U_Z + t + 1)
                act.activation(ZS[:, t, :], psum[:, t % 4, 0:L], ACT.Silu).then_inc(z_done, 1)
                if t % 2 == 0:
                    ahead(U_Z + t // 2)

            def token_copy(tile):
                act.wait_ge(xtr_ready, tile + 1)
                dst = XTOK[:, :, tile * P:(tile + 1) * P] if tile < 16 else BTOK[:, :, (tile - 16) * P:(tile - 15) * P]
                act.activation(dst, psum[:, (4, 6)[tile % 2], :].rearrange("p (b c) -> p b c", b=TB), ACT.Copy)\
                   .then_inc(xtr_done, 1)

            for tile in range(24):
                act.wait_ge(conv_done, tile + 1)
                bias = small("ssd_conv_b")[:, tile:tile + 1]
                if tile < 16:
                    dst, n = CV[:, tile % 2], T
                elif tile < 20:
                    dst, n = BF[:, tile - 16], T
                else:
                    dst, n = CF[:, tile - 20], L
                act.activation(dst[:, 0:n], CV[:, tile % 2, 0:n], ACT.Silu, bias=bias).then_inc(xbc_silu, 1)
                if tile % 2 == 0:
                    ahead(U_XBC + tile // 2)
                    if tile == 0:
                        act.wait_ge(acum_ready, 1)
                        act.activation(DEC, DEC, ACT.Exp).then_inc(dec_ready, 1)
                elif tile >= 3:
                    for old in (tile - 3, tile - 2):
                        if old < 20:
                            token_copy(old)

            with act.Fori(0, SG_) as g:
                for i in range(2):
                    act.wait_ge(st_ready, 4 * g + i + 1)
                    act.activation(S[:, i, :], psum[:, i, :], ACT.Copy).then_inc(s0_done, 1)
                for n in range(8):
                    act.wait_ge(sub_ready, 8 * g + n + 1)
                    act.activation(EX[:, n % 2, :], EX[:, n % 2, :], ACT.Exp).then_inc(ex_ready, 1)
            for t in range(16):
                act.wait_ge(yz_ready, 8)
                act.activation(SQ2[:, t, :], ZS[:, t, :], ACT.Square).then_inc(gsq_ready, 1)
            for g in range(SG_):
                act.wait_ge(gms_ready, g + 1)
                act.activation(RSTD[:, 0:L], RSTD[:, 0:L], ACT.Sqrt).then_inc(grms_ready, 1)
            for t in range(16):
                act.wait_ge(yf_ready, t + 1)
                act.activation(YNH[:, t, :], ZS[:, t, :], ACT.Copy).then_inc(yh_ready, 1)
            for n in range(U_SO, U_END):
                ahead(n)
            norm(3, L, so_added, lambda k: k + 1)

            for n in range(4):
                b, half = divmod(n, 2)
                act.wait_ge(htr_ready, n + 1)
                act.activation(TOKH[:, b, half * 512:(half + 1) * 512], psum[:, n, :], ACT.Copy).then_inc(htr_done, 1)
            act.wait_ge(topk_d, LB)
            act.activation(RSC[:, 10, 0:LB], RSC[:, 10, 0:LB], ACT.Exp).then_inc(topk_e, 1)

            def results(v):
                act.wait_ge(m_unit, UNITS * v + UNITS)
                for half in range(2):
                    act.activation(YE[:, half * 512:(half + 1) * 512], psum[:, 6 + half, :], ACT.Copy).then_inc(m_y, 1)

            def expert(v, first=False):
                for u in range(UNITS):
                    act.wait_ge(raw_ready[u % RAWS], 16 * (v * (UNITS // RAWS) + u // RAWS + 1))
                    if not first or u >= PAIRS or (not isinstance(v, int) or v):
                        act.wait_ge(m_unit, UNITS * v + u - PAIRS + 1)
                    act.activation(WH[u % PAIRS][:], raw[u % RAWS], ACT.Copy).then_inc(m_hi, 1)
                    if u == 1:
                        if not first:
                            results(v - 1)
                        for n in range(4):
                            act.wait_ge(m_gat, 4 * v + n + 1)
                            act.activation((HSH, HSL)[n // 2][:, 4 * (n % 2):4 * (n % 2) + 4, :],
                                           psum[:, n, :].rearrange("p (a b) -> p a b", a=4), ACT.Copy).then_inc(m_hs, 1)
                    p = u - PAIRS
                    if p >= 0 and p % 4 == 1 and p < 28:
                        j = p // 4
                        act.wait_ge(m_unit, UNITS * v + p + 1)
                        if j >= 2:
                            act.wait_ge(m_act, 7 * v + j - 1)
                        act.activation(SIL[:, j % 2, :], psum[:, 2 * (j % 2), :], ACT.Silu).then_inc(m_silu, 1)
                    if p >= 5 and p % 4 == 1 and p <= 29:
                        j = (p - 5) // 4
                        act.wait_ge(m_tr, 8 * v + j + 1)
                        act.activation(AEH[:, 4 * j:4 * j + 4, :], psum[:, 4 + j % 2, :].rearrange("p (a b) -> p a b", a=4),
                                       ACT.Copy).then_inc(m_trc, 1)
                    if p == 29:
                        act.wait_ge(m_tr, 8 * v + 8)
                        act.activation(GPT, psum[:, 5, 0:L], ACT.Copy).then_inc(m_trc, 1)

            expert(0, first=True)
            with act.Fori(1, NE) as e:
                expert(e)
            results(NE - 1)
            act.wait_ge(pos_ready, 1)
            most = act.value_load(flag[0:1, 0:1].bitcast(I32), min_val=0, max_val=L)
            with act.If(most > P):
                expert(NE, first=True)
                with act.Fori(1, NE) as e:
                    expert(e + NE)
                results(2 * NE - 1)
            norm(4, L, moe_added, lambda k: k + 1)

        @block.gpsimd
        def _(pool):
            steps = Tally(pool, pool_step)

            def fetch(c):
                pool.dma_start(ADAW, ada_w[1][:, :, c * 256:(c + 1) * 256]).then_inc(adw_in, 16)

            pool.wait_ge(cond_ready, 1)
            pool.wait_ge(ada_done, 12)
            fetch(0)
            for c in range(24):
                pool.wait_ge(adw_in, 16 * (c + 1))
                for s_ in ((1, 0) if c < 8 else (0,)):
                    prod = (ADAW, ADAP)[s_]
                    steps.step(pool.tensor_tensor(prod, ADAW, cond[:, :, s_:s_ + 1].broadcast_to([P, KD, 256]), ALU.mult))
                    for n in (4, 2):
                        steps.step(pool.tensor_tensor(prod[:, 0:n, :], prod[:, 0:n, :], prod[:, n:2 * n, :], ALU.add))
                    if c and (s_ == 1 or c >= 8):
                        pool.wait_ge(adc_folded, c)
                    last = pool.tensor_tensor(ADAC[:, s_, :], prod[:, 0, :], prod[:, 1, :], ALU.add)
                    if s_ == 1:
                        steps.step(last)
                last.then_inc(adc_ready, 1)
                pool.wait_ge(adc_ready, c + 1)
                if c < 23:
                    fetch(c + 1)
            pool.wait_ge(sw_ready, 1)
            pool.wait_ge(xtr_done, 16)
            pool.wait_ge(tile_done, 2 * U_SO)
            heads = lambda ap: ap.rearrange("p (h d) -> p h d", d=SPD)

            for g in range(SG_):
                for n, (blk, w) in enumerate(((0, None), (1, None), (2, None), (3, None), (2, None), (3, None))):
                    if n == 0:
                        pool.wait_ge(yd_ready, 4 * g)
                    pool.tensor_tensor(heads(XW[:, n, :]), heads(XTOK[:, blk, bass.ds(g * 512, 512)]),
                                       SW[:, n, bass.ds(g * REP, REP)].unsqueeze(2).broadcast_to([P, REP, SPD]),
                                       ALU.mult).then_inc(xw_ready, 1)

                def tri(n):
                    u, d = divmod(n, 2)
                    c, half = divmod(u, 2)
                    if n >= 2:
                        pool.wait_ge(seg_ready, 8 * g + n - 1)
                    pool.tensor_tensor(RT[:, n % 2, :].rearrange("p (h l) -> p h l", h=4),
                                       ident.unsqueeze(1).broadcast_to([P, 4, P]),
                                       ACUM[:, 2 * d + c, bass.ds(g * REP + 4 * half, 4)].unsqueeze(2).broadcast_to([P, 4, P]),
                                       ALU.mult).then_inc(rt_ready, 1)

                tri(0)
                tri(1)
                for n in range(4):
                    c, d = divmod(n, 2)
                    pool.tensor_tensor(heads(XD[:, n, :]), heads(XTOK[:, c, bass.ds(g * 512, 512)]),
                                       DTT[:, c, bass.ds(g * REP + SH * d, REP)].unsqueeze(2).broadcast_to([P, REP, SPD]),
                                       ALU.mult).then_inc(xw_ready, 1)
                for n in range(2, 8):
                    tri(n)
                    if n in (3, 7):
                        c = (n - 3) // 4
                        pool.wait_ge(y_ready, 2 * g + c)
                        pool.tensor_tensor(heads(XS), heads(XTOK[:, c, bass.ds(g * 512, 512)]),
                                           small("ssd_d")[:, bass.ds(g * REP, REP)].unsqueeze(2).broadcast_to([P, REP, SPD]),
                                           ALU.mult).then_inc(xs_ready, 1)

        @block.vector
        def _(dve):
            st = Tally(dve, dve_step)

            def norm(i, n):
                dve.wait_ge(ss_ready[i], 1)
                rs = RSTD[:, 0:n]
                dve.tensor_scalar(rs, psum[:, 6, 0:n], 1.0 / D, EPS, ALU.mult, ALU.add).then_inc(ms_ready[i], 1)
                dve.wait_ge(rms_ready[i], 1)
                st.step(dve.reciprocal(rs, rs))
                def low(k):
                    dve.wait_ge(hh_ready[i], k + 1)
                    dve.tensor_tensor(HTL[:, k, :], HT[:, k, :], HTH[:, k, :].bitcast(F32), ALU.subtract)\
                       .then_inc(hl_ready[i], 1)

                for k in range(KD):
                    dve.tensor_tensor(HT[:, k, 0:n], XT[:, k, 0:n], rs, ALU.mult).then_inc(hn_ready[i], 1)
                    if i in (1, 2) and k >= 2:
                        low(k - 2)
                if i in (1, 2):
                    low(KD - 2)
                    low(KD - 1)

            def split(q, r):
                dve.wait_ge(hi_done, 2 * q + r + 1)
                flat = "p k n -> p (k n)"
                dve.tensor_tensor(DWL[r][:].rearrange(flat), DRAW[r], DWH[r][:].rearrange(flat).bitcast(F32),
                                  ALU.subtract).then_inc(lo_done, 1)

            def ahead(n):
                if n + 2 < U_END:
                    split((n + 2) // 2, n % 2)

            def modulation(layer):
                wide_ = 48 if layer == 0 else 16
                if layer == 0:
                    dve.wait_ge(ada_folded, 12)
                else:
                    dve.wait_ge(adc_folded, 24)
                raw_ = psum[:, 7, 96 * layer:96 * layer + 96].rearrange("p (t s) -> p t s", s=2)
                bias = small("ada_b")[:, 48 * layer:48 * layer + 48].unsqueeze(2)
                st.inc(dve.tensor_tensor(MOD[:, layer, :, 0:1], raw_[:, :, 0:1], bias, ALU.add))
                st.step(dve.tensor_tensor(MOD[:, layer, 0:wide_, 1:2], raw_[:, 0:wide_, 1:2], bias[:, 0:wide_, :], ALU.add))
                for which in range(2):
                    i = 2 * layer + which
                    ns = 1 if i == 3 else 2
                    gain = small("norm_g")[:, 16 * which + 8 * layer:16 * which + 8 * layer + 8]
                    last = dve.scalar_tensor_tensor(GAIN[:, i, :, 0:ns], MOD[:, layer, 24 * which + 8:24 * which + 16, 0:ns],
                                                    1.0, gain.unsqueeze(2).broadcast_to([P, KD, ns]), ALU.add, ALU.mult)
                    if which == 0:
                        st.inc(last)
                last.then_inc(mod_ready, 1)
                dve.wait_ge(mod_ready, layer + 1)

            def residual(layer, which, k, src, streams):
                for s in range(streams):
                    cols = slice(s * L, (s + 1) * L)
                    last = dve.scalar_tensor_tensor(XT[:, k, cols], src[:, cols], MOD[:, layer, 24 * which + 16 + k, s:s + 1],
                                                    XT[:, k, cols], ALU.mult, ALU.add)
                return last

            def conv(dst, src, w, n):
                d3 = dst[:, 0:n].rearrange("p (s l) -> p s l", l=L)
                s3 = src[:, 0:n].rearrange("p (s l) -> p s l", l=L)
                st.step(dve.tensor_scalar(d3, s3, w[1], None, ALU.mult))
                st.step(dve.scalar_tensor_tensor(d3[:, :, 1:L], s3[:, :, 0:L - 1], w[0], d3[:, :, 1:L], ALU.mult, ALU.add))
                return dve.scalar_tensor_tensor(d3[:, :, 0:L - 1], s3[:, :, 1:L], w[2], d3[:, :, 0:L - 1],
                                                ALU.mult, ALU.add)

            dve.wait_ge(small_in, 32)
            dve.wait_ge(x_in, 16)
            norm(0, T)
            modulation(0)
            for k in range(KD):
                dve.wait_ge(hh_ready[0], k + 1)
                dve.tensor_tensor(HTL[:, k, :], HT[:, k, :], HTH[:, k, :].bitcast(F32), ALU.subtract)\
                   .then_inc(hl_ready[0], 1)
            split(0, 0)
            split(0, 1)
            for n in range(9):
                for t in range(2):
                    tile = 2 * n + t
                    i = tile % 4
                    if 4 <= tile < 8:
                        dve.wait_ge(tile_done, tile + 1)
                        dve.wait_ge(ha_done, i + 1)
                        dve.tensor_tensor(HA[:, i, :], psum[:, i, :], HA[:, i, :], ALU.mult).then_inc(gc_done, 1)
                        dve.wait_ge(gc_done, i + 1)
                        w = [small("ab_conv")[:, 4 * j + i:4 * j + i + 1] for j in range(3)]
                        st.step(conv(CV4[:, i, :], HA[:, i, :], w, T))
                    elif 8 <= tile < 12:
                        dve.wait_ge(tile_done, tile + 1)
                        dve.tensor_tensor(CV4[:, i, :], psum[:, i, :], CV4[:, i, :], ALU.mult).then_inc(gb_done, 1)
                    if t == 0:
                        ahead(n)
            dve.wait_ge(rope_in, 16)
            for t in range(5):
                x = Q[:, t, 0:L] if t < 4 else KK[:, 0, 0:L]
                dve.wait_ge(rot_ready, t + 1)
                if t:
                    dve.wait_ge(rope_done, t)
                st.inc(dve.tensor_tensor(rtmp, psum[:, 4 + t % 2, 0:L], sinT, ALU.mult))
                st.step(dve.tensor_tensor(x, x, cosT, ALU.mult))
                dve.tensor_tensor(x, x, rtmp, ALU.add).then_inc(rope_done, 1)
            dve.wait_ge(rope_done, 5)
            st.inc(dve.tensor_copy(KK[0:HD, 1, :], KK[HD:P, 0, :]))
            st.step(dve.tensor_copy(KK[HD:P, 1, :], KK[HD:P, 0, :]))
            dve.tensor_copy(KK[HD:P, 0, :], KK[0:HD, 0, :]).then_inc(kk_ready, 1)

            for t in range(4):
                dve.wait_ge(cat_hi, t + 1)
                dve.tensor_tensor(CATL[:, t, :], CV4[:, t, :], CATH[:, t, :].bitcast(F32), ALU.subtract).then_inc(cat_lo, 1)

            steps0 = st.n
            per_g = 16 * 3
            with dve.Fori(0, NKV) as g:
                st.n = steps0 + per_g * g
                for s in range(16 + 1):
                    if s < 16:
                        hh, qb = divmod(s, TB)
                        b = s % 3
                        dve.wait_ge(sc_ready, 16 * g + s + 1)
                        if s >= 3:
                            dve.wait_ge(pt_ready, 16 * g + s - 2)
                        k0 = 0 if qb < LB else L
                        src = psum[:, 4 + s % 2, k0:T]
                        if qb < LB:
                            dve.scalar_tensor_tensor(SS[:, b, :], src, HD ** -0.5, smask[:, qb, :], ALU.mult, ALU.add)\
                               .then_inc(sc_used, 1)
                        else:
                            dve.tensor_scalar(SS[:, b, k0:T], src, HD ** -0.5, None, ALU.mult).then_inc(sc_used, 1)
                        dve.wait_ge(sc_used, 16 * g + s + 1)
                        st.step(dve.reduce_max(att_s[:, 0, b:b + 1], SS[:, b, k0:T], AX_X))
                        dve.tensor_scalar(att_s[:, 1, b:b + 1], att_s[:, 0, b:b + 1],
                                              small("sink")[:, bass.ds(4 * g + hh, 1)], -1.0, ALU.max, ALU.mult)\
                               .then_inc(nm_ready, 1)
                    u = s - 1
                    if u >= 0:
                        b = u % 3
                        k0 = 0 if u % TB < LB else L
                        dve.wait_ge(exp_ready, 32 * g + 2 * u + 2)
                        st.step(dve.tensor_tensor(att_s[:, 4, b:b + 1], att_s[:, 2, b:b + 1], att_s[:, 3, b:b + 1], ALU.add))
                        st.step(dve.reciprocal(att_s[:, 5, b:b + 1], att_s[:, 4, b:b + 1]))
                        dve.tensor_scalar(SS[:, b, k0:T], SS[:, b, k0:T], att_s[:, 5, b:b + 1], None, ALU.mult)\
                           .then_inc(pn_ready, 1)
                for i in range(2):
                    dve.wait_ge(att_out, 2 * g + i + 1)
                    dve.tensor_tensor(CATL[:, 4 + 2 * g + i, :], psum[:, i, :], CATH[:, 4 + 2 * g + i, :].bitcast(F32),
                                      ALU.subtract).then_inc(att_lo, 1)
            st.n = steps0 + per_g * NKV

            for k in range(KD):
                if k % 2 == 1:
                    ahead(U_OUT + k // 2)
                dve.wait_ge(tile_done, 2 * U_OUT + k + 1)
                residual(0, 0, k, psum[:, (2 * U_OUT + k) % 4, :], 2).then_inc(abo_added, 1)
            norm(1, T)

            def gated_up(i):
                split(i + U_GU // 2 + 1, 1)
                for t in range(2):
                    dve.wait_ge(tile_done, 2 * U_GU + 4 * i + t + 3)
                    dve.wait_ge(gate_done, 2 * i + t + 1)
                    dve.tensor_tensor(GS[:, t, :], psum[:, t, :], GS[:, t, :], ALU.mult).then_inc(f_ready, 1)
                    if t == 0:
                        split(i + U_GU // 2 + 2, 0)
                for t in range(2):
                    dve.wait_ge(fh_done, 2 * i + t + 1)
                    dve.tensor_tensor(ATL[:, 2 * i + t, :], GS[:, t, :], ATH[:, 2 * i + t, :].bitcast(F32), ALU.subtract)\
                       .then_inc(ff_done, 1)

            gated_up(0)
            with dve.Fori(1, 11) as i:
                gated_up(i)
            for k in range(KD):
                if k % 2 == 0:
                    ahead(U_DOWN + 3 * (k // 2))
                    ahead(U_DOWN + 3 * (k // 2) + 1)
                    if k == 6:
                        modulation(1)
                    ahead(U_DOWN + 3 * (k // 2) + 2)
                dve.wait_ge(tile_done, 2 * U_DOWN + 6 * (k // 2) + 5 + k % 2)
                residual(0, 1, k, psum[:, k % 4, :], 2).then_inc(dn_added, 1)
            norm(2, T)
            ahead(U_DT)

            r, e_, z, z2 = (DTMP[:, i, :] for i in range(4))
            blocks = lambda ap: ap.rearrange("p (b h) -> p b h", b=TB)
            dtf = DTT.rearrange("p b h -> p (b h)")
            daf = DA.rearrange("p b h -> p (b h)")
            dve.wait_ge(tile_done, 2 * U_DT + 2)
            st.step(dve.tensor_tensor(blocks(r), blocks(psum[:, 5, 0:TB * 64]),
                                      small("dt_bias").unsqueeze(1).broadcast_to([P, TB, 64]), ALU.add))
            dve.scalar_tensor_tensor(e_, r, -1.0, r, ALU.mult, ALU.min).then_inc(dt_exp_in, 1)
            dve.wait_ge(dt_exp, 2)
            st.step(dve.tensor_scalar(z, e_, 2.0, None, ALU.add))
            st.step(dve.reciprocal(z, z))
            st.step(dve.tensor_tensor(z, z, e_, ALU.mult))
            st.step(dve.tensor_tensor(z2, z, z, ALU.mult))
            st.step(dve.tensor_scalar(e_, z2, 1.0 / 15, None, ALU.mult))
            for n in (13, 11, 9, 7, 5, 3):
                st.step(dve.scalar_tensor_tensor(e_, e_, 1.0 / n, z2, ALU.add, ALU.mult))
            st.step(dve.scalar_tensor_tensor(e_, e_, 1.0, z, ALU.add, ALU.mult))
            st.step(dve.tensor_scalar(r, r, 0.0, None, ALU.max))
            st.inc(dve.scalar_tensor_tensor(dtf, e_, 2.0, r, ALU.mult, ALU.add))
            st.step(dve.tensor_scalar(NEGA, NEGA, -1.0, None, ALU.mult))
            dve.tensor_tensor(DA, DTT, NEGA.unsqueeze(1).broadcast_to([P, TB, 64]), ALU.mult).then_inc(a_ready, 1)

            for i in range(8):
                ahead(U_Z + i)

            def conv_tile(tile):
                dve.wait_ge(tile_done, 2 * U_XBC + tile + 1)
                if tile in range(2, 18):
                    dve.wait_ge(xtr_ready, tile - 1)
                elif tile >= 18:
                    dve.wait_ge(xbc_silu, tile - 1)
                w = [small("ssd_conv")[:, 24 * i + tile:24 * i + tile + 1] for i in range(3)]
                conv(CV[:, tile % 2], psum[:, tile % 4, :], w, T if tile < 20 else L).then_inc(conv_done, 1)
                if tile % 2 == 0:
                    ahead(U_XBC + tile // 2)

            conv_tile(0)
            dve.wait_ge(dec_raw, 1)
            st.step(dve.tensor_copy(ACUM, psum[:, 7, 0:12 * SH].rearrange("p (a b) -> p a b", a=12)))
            st.inc(dve.tensor_copy(DEC[:, 0:4, :], ACUM[:, 0:4, :]))
            st.inc(dve.tensor_copy(DEC[:, 6:8, :], ACUM[:, 4:6, :]))
            for n, (total, own) in enumerate(((4, 0), (5, 3), (10, 6), (10, 7), (11, 8), (11, 9))):
                last = dve.tensor_tensor(DEC[:, (4, 5, 8, 9, 10, 11)[n], :], ACUM[:, total, :], ACUM[:, own, :], ALU.subtract)
                if n < 5:
                    st.inc(last)
            last.then_inc(acum_ready, 1)
            dve.wait_ge(dec_ready, 1)
            for n, (col, blk, h0) in enumerate(((4, 0, 0), (5, 1, SH), (8, 2, 0), (9, 3, 0), (10, 2, SH), (11, 3, SH))):
                last = dve.tensor_tensor(SW[:, n, :], DEC[:, col, :], DTT[:, blk, h0:h0 + SH], ALU.mult)
                if n < 5:
                    st.inc(last)
            last.then_inc(sw_ready, 1)
            for tile in range(1, 24):
                conv_tile(tile)

            heads = lambda ap: ap.rearrange("p (h d) -> p h d", d=SPD)

            def per_head(col, g):
                return DEC[:, col, bass.ds(g * REP, REP)].unsqueeze(2).broadcast_to([P, REP, SPD])

            steps1 = st.n
            with dve.Fori(0, SG_) as g:
                st.n = steps1 + 12 * g
                for i in range(2):
                    dve.wait_ge(s0_done, 2 * g + i + 1)
                    st.step(dve.tensor_tensor(heads(S[:, 2 + i, :]), heads(S[:, i, :]), per_head(6 + i, g), ALU.mult))
                    dve.wait_ge(st_ready, 4 * g + 3 + i)
                    dve.tensor_tensor(S[:, 2 + i, :], S[:, 2 + i, :], psum[:, 2 + i, :], ALU.add).then_inc(s1_done, 1)
                dve.wait_ge(cb_ready, g + 1)
                for d, m in enumerate(("le", "ge")):
                    st.inc(dve.tensor_tensor(CBM[:, :, d, :], psum[:, 4, 0:2 * P].rearrange("p (c l) -> p c l", c=2),
                                             const(m).unsqueeze(1).broadcast_to([P, 2, P]), ALU.mult))
                dve.wait_ge(dve_step, st.n)

                def between(n):
                    u, d = divmod(n, 2)
                    c, half = divmod(u, 2)
                    dve.wait_ge(seg_ready, 8 * g + n + 1)
                    if n >= 2:
                        dve.wait_ge(mm_ready, 8 * g + n - 1)
                    for h in range(4):
                        last = dve.tensor_scalar(EX[:, n % 2, h * P:(h + 1) * P], psum[:, 5 + n % 2, h * P:(h + 1) * P],
                                                 ACUM[:, 2 * d + c, bass.ds(g * REP + 4 * half + h, 1)], 0.0,
                                                 ALU.subtract, ALU.min)
                    last.then_inc(sub_ready, 1)

                def decayed(n):
                    u, d = divmod(n, 2)
                    dve.wait_ge(ex_ready, 8 * g + n + 1)
                    if u >= 2:
                        dve.wait_ge(yd_ready, 4 * g + u - 1)
                    dve.tensor_tensor(MM[:, u % 2, d, :].rearrange("p (h l) -> p h l", h=4),
                                      EX[:, n % 2, :].rearrange("p (h l) -> p h l", h=4),
                                      CBM[:, u // 2, d, :].unsqueeze(1).broadcast_to([P, 4, P]), ALU.mult)\
                       .then_inc(mm_ready, 1)
                    if n < 6:
                        between(n + 2)

                def combine(c):
                    dve.wait_ge(yo_ready, 2 * g + c + 1)
                    if c:
                        dve.wait_ge(ytr_ready, 2 * g + 1)
                    st.inc(dve.tensor_tensor(heads(YT[:, 0, :]), heads(psum[:, 0, :]), per_head(c, g), ALU.mult))
                    st.step(dve.tensor_tensor(heads(YT[:, 1, :]), heads(psum[:, 1, :]), per_head(2 + c, g), ALU.mult))
                    st.step(dve.tensor_tensor(YT[:, 0, :], YT[:, 0, :], YT[:, 1, :], ALU.add))
                    dve.wait_ge(xs_ready, 2 * g + c + 1)
                    st.step(dve.tensor_tensor(YT[:, 0, :], YT[:, 0, :], XS, ALU.add))
                    dve.wait_ge(yd_ready, 4 * g + 2 * c + 2)
                    dve.tensor_tensor(YT[:, 0, :], YT[:, 0, :], psum[:, 2 + c, :], ALU.add).then_inc(y_ready, 1)

                def gated(c):
                    dve.wait_ge(ytr_ready, 2 * g + c + 1)
                    zs = ZS[:, bass.ds(4 * g, 4), c * P:(c + 1) * P]
                    dve.tensor_tensor(zs, psum[:, 7, :].rearrange("p (t l) -> p t l", t=4), zs, ALU.mult)\
                       .then_inc(yz_ready, 1)

                between(0)
                between(1)
                for n in range(5):
                    decayed(n)
                combine(0)
                for n in range(5, 8):
                    decayed(n)
                gated(0)
                combine(1)
                gated(1)
            st.n = steps1 + 12 * SG_

            for g in range(SG_):
                dve.wait_ge(gss_ready, g + 1)
                dve.wait_ge(yf_ready, 4 * g)
                rs = RSTD[:, 0:L]
                dve.tensor_scalar(rs, psum[:, 4 + g % 2, 0:L], 1.0 / 512, EPS, ALU.mult, ALU.add).then_inc(gms_ready, 1)
                dve.wait_ge(grms_ready, g + 1)
                st.step(dve.reciprocal(rs, rs))
                for t in range(4):
                    i = 4 * g + t
                    dve.scalar_tensor_tensor(ZS[:, i, :], ZS[:, i, :], small("ssd_norm_g")[:, i:i + 1], rs,
                                             ALU.mult, ALU.mult).then_inc(yf_ready, 1)
            for i in range(16):
                dve.wait_ge(yh_ready, i + 1)
                dve.tensor_tensor(YNL[:, i, :], ZS[:, i, :], YNH[:, i, :].bitcast(F32), ALU.subtract).then_inc(yn_ready, 1)
            for k in range(KD):
                if k % 2 == 0:
                    ahead(U_SO + k)
                    ahead(U_SO + k + 1)
                dve.wait_ge(tile_done, 2 * U_SO + 4 * (k // 2) + 3 + k % 2)
                residual(1, 0, k, psum[:, k % 4, :], 1).then_inc(so_added, 1)
            norm(3, L)

            for n in range(4):
                b, half = divmod(n, 2)
                cols = slice(half * 512, (half + 1) * 512)
                dve.wait_ge(htr_done, n + 1)
                dve.tensor_tensor(TOKL[:, b, cols], psum[:, n, :], TOKH[:, b, cols].bitcast(F32), ALU.subtract)\
                   .then_inc(htl_done, 1)

            dve.wait_ge(lg_raw, 1)
            st.step(dve.tensor_copy(LG, psum[:, 7, 0:LB * NE].rearrange("p (b e) -> p b e", b=LB)))
            st.inc(dve.memset(ASG, 0.0))
            st.inc(dve.memset(GATE, 0.0))
            st.inc(dve.memset(POS, 0.0))
            for b in range(LB):
                m0, eq, cs, sel0, l2, m1, sel1 = (RSC[:, i, :] for i in (0, 1, 2, 3 + b, 5, 6, 7 + b))
                for m, l, sel in ((m0, LG[:, b, :], sel0), (m1, l2, sel1)):
                    st.step(dve.max(m, l))
                    st.step(dve.tensor_scalar(eq, l, m[:, 0:1], None, ALU.is_equal))
                    st.step(dve.tensor_tensor_scan(cs, ones[:, 0:NE], eq, 0.0, ALU.mult, ALU.add))
                    st.step(dve.scalar_tensor_tensor(sel, cs, 1.0, eq, ALU.is_equal, ALU.mult))
                    if sel is sel0:
                        st.step(dve.scalar_tensor_tensor(l2, sel, -3.0e38, l, ALU.mult, ALU.add))
                last = dve.tensor_tensor(RSC[:, 10, b:b + 1], m1[:, 0:1], m0[:, 0:1], ALU.subtract)
                last.then_inc(topk_d, 1)
                dve.tensor_tensor(ASG[:, b, 0:NE], sel0, sel1, ALU.add).then_inc(asg_ready, 1)
                dve.wait_ge(asg_ready, b + 1)
            st.inc(dve.tensor_scalar(iota_hi, const("iota"), float(P), None, ALU.add))
            for n in range(4):
                dve.memset(ACC[:, 2 * n:2 * n + 2, :], 0.0).then_inc(m_acc, 1)
            dve.wait_ge(topk_e, 1)
            ed, w0, w1 = RSC[:, 10, 0:LB], RSC[:, 9, 0:LB], RSC[:, 11, 0:LB]
            st.step(dve.tensor_scalar(w0, ed, 1.0, None, ALU.add))
            st.step(dve.reciprocal(w0, w0))
            st.step(dve.tensor_tensor(w1, ed, w0, ALU.mult))
            for b in range(LB):
                st.step(dve.tensor_scalar(GATE[:, b, 0:NE], RSC[:, 3 + b, :], w0[:, b:b + 1], None, ALU.mult))
                st.step(dve.scalar_tensor_tensor(GATE[:, b, 0:NE], RSC[:, 7 + b, :], w1[:, b:b + 1], GATE[:, b, 0:NE],
                                                 ALU.mult, ALU.add))
            dve.wait_ge(pos_raw, 1)
            st.inc(dve.tensor_copy(POS[:, :, 0:NE], psum[:, 6, 0:LB * NE].rearrange("p (b e) -> p b e", b=LB)))
            st.step(dve.reduce_max(CNT[:, 0:1], psum[:, 6, 2 * NE:3 * NE], AX_X))
            dve.tensor_copy(flag[:, 0:1].bitcast(I32), CNT[:, 0:1]).then_inc(pos_ready, 1)

            def one_hot(iota, e, gathers):
                if not isinstance(gathers, int) or gathers:
                    dve.wait_ge(m_gat, 4 * gathers)
                for b in range(LB):
                    last = dve.tensor_scalar(PM[:, b, :], iota, POS[:, b, bass.ds(e, 1)], ASG[:, b, bass.ds(e, 1)],
                                             ALU.is_equal, ALU.mult)
                last.then_inc(m_p, 1)

            def add_results(v):
                for n in range(4):
                    dve.wait_ge(m_sc, 4 * v + n + 1)
                    acc = ACC[:, 2 * n:2 * n + 2, :]
                    dve.tensor_tensor(acc, psum[:, 4 + n, :].rearrange("p (a b) -> p a b", a=2), acc, ALU.add)\
                       .then_inc(m_acc, 1)

            def expert(e, v, iota, first=False):
                for u in range(UNITS):
                    dve.wait_ge(m_hi, UNITS * v + u + 1)
                    dve.tensor_tensor(WL[u % PAIRS][:], raw[u % RAWS], WH[u % PAIRS][:].bitcast(F32), ALU.subtract)\
                       .then_inc(m_lo, 1)
                    if u == 2 and not first:
                        dve.wait_ge(m_acc, 4 * v)
                        add_results(v - 1)
                    if u == 9:
                        dve.wait_ge(m_tr, 8 * v)
                        for b in range(LB):
                            last = dve.tensor_scalar(GP[:, b, :], iota, POS[:, b, bass.ds(e, 1)], GATE[:, b, bass.ds(e, 1)],
                                                     ALU.is_equal, ALU.mult)
                        last.then_inc(m_gp, 1)
                    if u == 12:
                        one_hot(iota, e + 1, v + 1)
                    p = u - PAIRS
                    if p >= 0 and p % 4 == 3 and p < 28:
                        j = p // 4
                        dve.wait_ge(m_unit, UNITS * v + p + 1)
                        dve.wait_ge(m_silu, 7 * v + j + 1)
                        if j >= 2:
                            dve.wait_ge(m_tr, 8 * v + j - 1)
                        dve.tensor_tensor(AC[:, j % 2, :], psum[:, 2 * (j % 2) + 1, :], SIL[:, j % 2, :], ALU.mult)\
                           .then_inc(m_act, 1)
                    if p >= 5 and p % 4 == 1 and p <= 29:
                        j = (p - 5) // 4
                        dve.wait_ge(m_trc, 8 * v + j + 1)
                        dve.tensor_tensor(AEL[:, 4 * j:4 * j + 4, :], psum[:, 4 + j % 2, :].rearrange("p (a b) -> p a b", a=4),
                                          AEH[:, 4 * j:4 * j + 4, :].bitcast(F32), ALU.subtract).then_inc(m_ael, 1)

            dve.wait_ge(pos_ready, 1)
            one_hot(const("iota"), 0, 0)
            expert(0, 0, const("iota"), first=True)
            with dve.Fori(1, NE) as e:
                expert(e, e, const("iota"))
            dve.wait_ge(m_acc, 4 * NE)
            add_results(NE - 1)
            most = dve.value_load(flag[0:1, 0:1].bitcast(I32), min_val=0, max_val=L)
            with dve.If(most > P):
                one_hot(iota_hi, 0, NE)
                expert(0, NE, iota_hi, first=True)
                with dve.Fori(1, NE) as e:
                    expert(e, e + NE, iota_hi)
                dve.wait_ge(m_acc, 8 * NE)
                add_results(2 * NE - 1)
                dve.wait_ge(m_acc, 8 * NE + 4)
            dve.wait_ge(m_acc, 4 * NE + 4)
            for k in range(KD):
                residual(1, 1, k, ACC[:, k, :], 1).then_inc(moe_added, 1)
            norm(4, L)


def constants():
    t = np.arange(P)
    c = np.zeros((P, NCONST), np.float32)

    def put(name, m):
        o, n = CONST[name]
        c[:, o:o + n] = m

    put("ident", np.eye(P))
    put("ones", 1.0)
    put("le", t[:, None] <= t[None, :])
    put("ge", t[:, None] >= t[None, :])
    put("lt", t[:, None] < t[None, :])
    put("gt", t[:, None] > t[None, :])
    put("iota", t[None, :])
    rot = np.zeros((P, P), np.float32)
    for f in range(P):
        if f % 32 < ROPE_PAIRS:
            rot[f + ROPE_PAIRS, f] = -1.0
        else:
            rot[f - ROPE_PAIRS, f] = 1.0
    put("rot", rot)
    tok = np.arange(L)
    inv = (np.float32(10000.0) ** (-np.arange(ROPE_PAIRS, dtype=np.float32) / np.float32(ROPE_PAIRS))).astype(np.float32)
    f = np.arange(P) % HD
    where = np.where((f // 32)[:, None] == 0, (tok // GRID_W)[None, :], (tok % GRID_W)[None, :]).astype(np.float32)
    ang = where * inv[f % ROPE_PAIRS][:, None]
    q, k = np.arange(L), np.arange(L)
    mask = np.zeros((L, T), np.float32)
    mask[:, :L] = np.where(np.abs(q[:, None] - k[None, :]) <= WINDOW, 0.0, NEG)
    rope = np.concatenate([np.cos(ang), np.sin(ang), mask[:P], mask[P:]], axis=1).astype(np.float32)
    return c, np.ascontiguousarray(rope)


WEIGHTS = ["ada_w", "ab_w_in", "ab_w_out", "ffn_w_gate", "ffn_w_up", "ffn_w_down", "ssd_w_in", "ssd_w_out",
           "moe_w_gate", "moe_w_up", "moe_w_down"]


def lay_out(inputs):
    g = {k: np.asarray(v) for k, v in inputs.items()}

    def cols(v):
        v = v.reshape(-1, v.shape[-1] // P, P)
        return v.transpose(2, 0, 1).reshape(P, -1)

    def rows(*v):
        v = np.concatenate([x.reshape(-1) for x in v])
        return np.broadcast_to(v, (P, v.size))

    parts = {
        "c": np.stack([g["c"][0].reshape(KD, P).T, g["c_ctx"].reshape(KD, P).T], axis=2).reshape(P, 16),
        "ada_b": cols(g["ada_b"]),
        "norm_g": np.concatenate([cols(g["norm1_g"]), cols(g["norm2_g"])], axis=1),
        "final_g": cols(g["final_g"]),
        "ab_conv": cols(g["ab_conv_w"][0]),
        "ssd_conv": cols(g["ssd_conv_w"][0]),
        "ssd_conv_b": cols(g["ssd_conv_b"]),
        "ssd_norm_g": cols(g["ssd_norm_g"]),
        "router": g["moe_router"][0].reshape(KD, P, NE).transpose(1, 0, 2).reshape(P, -1),
        "sink": rows(g["ab_sink"]),
        "dt_bias": rows(g["ssd_dt_bias_f"], g["ssd_dt_bias_b"]),
        "a_log": rows(g["ssd_a_log_f"], g["ssd_a_log_b"]),
        "ssd_d": rows(g["ssd_d"]),
    }
    arrays = {"smalls": np.ascontiguousarray(np.concatenate([parts[k] for k in SMALL], axis=1))}
    arrays["xT"] = np.ascontiguousarray(np.concatenate([g["x"][0].T, g["ctx"][0].T], axis=1))
    arrays["consts"], arrays["rope"] = constants()
    for k in WEIGHTS:
        arrays[k] = np.ascontiguousarray(g[k])
    return arrays


def kernel(**inputs):
    import concourse.bacc as bacc
    from concourse.bass_utils import run_bass_kernel_spmd

    arrays = lay_out(inputs)
    nc = bacc.Bacc("TRN2", target_bir_lowering=False, num_devices=1)
    aps = {k: nc.dram_tensor(k, v.shape, mybir.dt.from_np(v.dtype), kind="ExternalInput").ap() for k, v in arrays.items()}
    out = nc.dram_tensor("outT", (D, L), F32, kind="ExternalOutput").ap()
    build(nc, aps, out)
    r = run_bass_kernel_spmd(nc, [arrays], core_ids=[0])
    return np.ascontiguousarray(r.results[0]["outT"].T)[None]
```
